# Optimizing a Trainium2 kernel written in Bass

```python
import jax, jax.numpy as jnp
from jax import lax
import numpy as np

D_MODEL = 2048
BATCH = 1
SEQ = 256
DEPTH = 2

CHUNK = 64
N_PREV_CHUNKS = 8
N_BAND = N_PREV_CHUNKS + 1
A_HEADS = 8
A_HEAD_DIM = 128
A_WIDTH = A_HEADS * A_HEAD_DIM
REL_CLIP = 256
R_HEADS = 8
R_HEAD_DIM = 128
R_WIDTH = R_HEADS * R_HEAD_DIM
ROPE_BASE = 10000.0
N_BRANCH = 2
D_FF = 5632
CONV_W = 3
EPS = 1e-6

IN_SIZES = (A_WIDTH, A_WIDTH, A_WIDTH,
            R_WIDTH, R_WIDTH, R_WIDTH, R_WIDTH,
            N_BRANCH * D_MODEL)
D_IN = sum(IN_SIZES)
IN_SPLITS = [int(s) for s in np.cumsum(IN_SIZES)[:-1]]

kernel_name = "hybrid_chunked_attn_retention_convffn"

def rmsnorm(x, g):
    xf = x.astype(jnp.float32)
    y = xf * lax.rsqrt(jnp.mean(xf * xf, axis=-1, keepdims=True) + EPS)
    return (y * g.astype(jnp.float32)).astype(x.dtype)

def rotary(x):
    _, s, _, d = x.shape
    half = d // 2
    inv = ROPE_BASE ** (-jnp.arange(half, dtype=jnp.float32) / half)
    ang = jnp.arange(s, dtype=jnp.float32)[:, None] * inv[None, :]
    cos = jnp.cos(ang)[None, :, None, :]
    sin = jnp.sin(ang)[None, :, None, :]
    xf = x.astype(jnp.float32)
    x1, x2 = xf[..., :half], xf[..., half:]
    return jnp.concatenate([x1 * cos - x2 * sin, x1 * sin + x2 * cos], axis=-1).astype(x.dtype)

def chunked_band_attention(q, k, v, rel_bias):
    b, s, h, hd = q.shape
    nc = s // CHUNK
    qc = q.reshape(b, nc, CHUNK, h, hd)
    pad = ((0, 0), (N_PREV_CHUNKS, 0), (0, 0), (0, 0), (0, 0))
    kp = jnp.pad(k.reshape(b, nc, CHUNK, h, hd), pad)
    vp = jnp.pad(v.reshape(b, nc, CHUNK, h, hd), pad)
    scale = hd ** -0.5
    scores = jnp.stack(
        [jnp.einsum('bcqhd,bckhd->bhcqk', qc, kp[:, j:j + nc]) for j in range(N_BAND)],
        axis=4).astype(jnp.float32) * scale
    i_idx = np.arange(CHUNK)[:, None, None]
    j_idx = np.arange(N_BAND)[None, :, None]
    l_idx = np.arange(CHUNK)[None, None, :]
    dist = (N_PREV_CHUNKS - j_idx) * CHUNK + i_idx - l_idx
    idx = np.clip(dist, -REL_CLIP, REL_CLIP) + REL_CLIP
    bias = rel_bias[:, idx].astype(jnp.float32)
    scores = scores + bias[None, :, None]
    valid = (jnp.arange(nc)[:, None] - N_PREV_CHUNKS + jnp.arange(N_BAND)[None, :]) >= 0
    scores = jnp.where(valid[None, None, :, None, :, None], scores, -jnp.inf)
    p = jax.nn.softmax(scores.reshape(b, h, nc, CHUNK, N_BAND * CHUNK), axis=-1)
    p = p.reshape(b, h, nc, CHUNK, N_BAND, CHUNK).astype(v.dtype)
    out = jnp.einsum('bhcqk,bckhd->bcqhd', p[:, :, :, :, 0], vp[:, 0:nc])
    for j in range(1, N_BAND):
        out = out + jnp.einsum('bhcqk,bckhd->bcqhd', p[:, :, :, :, j], vp[:, j:j + nc])
    return out.reshape(b, s, h * hd)

def retention(q, k, v):
    b, s, h, d = q.shape
    nc = s // CHUNK
    f32 = jnp.float32
    qc = q.astype(f32).reshape(b, nc, CHUNK, h, d)
    kc = (k.astype(f32) * d ** -0.5).reshape(b, nc, CHUNK, h, d)
    vc = v.astype(f32).reshape(b, nc, CHUNK, h, d)
    lg = jnp.log1p(-jnp.exp2(-5.0 - jnp.arange(h, dtype=f32)))
    n = jnp.arange(CHUNK, dtype=f32)
    diff = n[:, None] - n[None, :]
    dmat = jnp.where(diff >= 0, jnp.exp(lg[:, None, None] * jnp.maximum(diff, 0.0)), 0.0)
    inner = jnp.einsum('bcnhd,bcmhd->bhcnm', qc, kc) * dmat[None, :, None]
    y_in = jnp.einsum('bhcnm,bcmhe->bcnhe', inner, vc)
    zeta = jnp.exp(lg[:, None] * (CHUNK - 1 - n)[None, :])
    kv = jnp.einsum('bcmhd,bcmhe,hm->cbhde', kc, vc, zeta)
    chunk_decay = jnp.exp(lg * CHUNK)[None, :, None, None]

    def step(state, kv_c):
        return state * chunk_decay + kv_c, state

    _, r_prev = lax.scan(step, jnp.zeros((b, h, d, d), f32), kv)
    xi = jnp.exp(lg[:, None] * (n + 1.0)[None, :])
    y_x = jnp.einsum('bcnhd,cbhde,hn->bcnhe', qc, r_prev, xi)
    return (y_in + y_x).reshape(b, s, h, d).astype(q.dtype)

def causal_depthwise_conv(u, w, bias):
    s = u.shape[1]
    up = jnp.pad(u, ((0, 0), (CONV_W - 1, 0), (0, 0)))
    out = bias
    for t in range(CONV_W):
        out = out + w[t] * up[:, t:t + s]
    return out

def setup_inputs(seed: int = 0) -> dict:
    key = jax.random.key(seed)
    ks = jax.random.split(key, 16)
    f32 = jnp.float32
    nrm = lambda k, shape, sc: jax.random.normal(k, shape, f32) * sc
    return {
        "x": nrm(ks[0], (BATCH, SEQ, D_MODEL), 1.0),
        "w_in": nrm(ks[1], (DEPTH, D_MODEL, D_IN), D_MODEL ** -0.5),
        "w_br": nrm(ks[2], (DEPTH, N_BRANCH, A_WIDTH, D_MODEL), A_WIDTH ** -0.5),
        "w_o": nrm(ks[3], (DEPTH, D_MODEL, D_MODEL), D_MODEL ** -0.5),
        "mix_norm": 1.0 + nrm(ks[4], (DEPTH, D_MODEL), 0.02),
        "q_gain": 1.0 + nrm(ks[5], (DEPTH, A_HEAD_DIM), 0.02),
        "k_gain": 1.0 + nrm(ks[6], (DEPTH, A_HEAD_DIM), 0.02),
        "rel_bias": nrm(ks[7], (A_HEADS, 2 * REL_CLIP + 1), 0.5),
        "r_gain": 1.0 + nrm(ks[8], (DEPTH, R_HEAD_DIM), 0.02),
        "ffn_norm": 1.0 + nrm(ks[9], (DEPTH, D_MODEL), 0.02),
        "w_up": nrm(ks[10], (DEPTH, D_MODEL, 2 * D_FF), D_MODEL ** -0.5),
        "conv_w": nrm(ks[11], (DEPTH, CONV_W, 2 * D_FF), CONV_W ** -0.5),
        "conv_b": nrm(ks[12], (DEPTH, 2 * D_FF), 0.01),
        "w_down": nrm(ks[13], (DEPTH, D_FF, D_MODEL), D_FF ** -0.5),
    }

def reference(x, w_in, w_br, w_o, mix_norm, q_gain, k_gain, rel_bias, r_gain,
              ffn_norm, w_up, conv_w, conv_b, w_down):
    b, s, _ = x.shape
    for l in range(DEPTH):
        h = rmsnorm(x, mix_norm[l])
        z = h @ w_in[l]
        aq, ak, av, rq, rk, rv, rg, gl = jnp.split(z, IN_SPLITS, axis=-1)
        aq = rmsnorm(aq.reshape(b, s, A_HEADS, A_HEAD_DIM), q_gain[l])
        ak = rmsnorm(ak.reshape(b, s, A_HEADS, A_HEAD_DIM), k_gain[l])
        av = av.reshape(b, s, A_HEADS, A_HEAD_DIM)
        ya = chunked_band_attention(aq, ak, av, rel_bias)
        rq = rotary(rq.reshape(b, s, R_HEADS, R_HEAD_DIM))
        rk = rotary(rk.reshape(b, s, R_HEADS, R_HEAD_DIM))
        rv = rv.reshape(b, s, R_HEADS, R_HEAD_DIM)
        yr = rmsnorm(retention(rq, rk, rv), r_gain[l]).reshape(b, s, R_WIDTH)
        yr = jax.nn.silu(rg) * yr
        gates = jax.nn.sigmoid(gl.reshape(b, s, N_BRANCH, D_MODEL))
        merged = gates[:, :, 0] * (ya @ w_br[l, 0]) + gates[:, :, 1] * (yr @ w_br[l, 1])
        x = x + merged @ w_o[l]
        h = rmsnorm(x, ffn_norm[l])
        u = causal_depthwise_conv(h @ w_up[l], conv_w[l], conv_b[l])
        ua, ub = jnp.split(u, 2, axis=-1)
        x = x + (jax.nn.gelu(ua, approximate=False) * ub) @ w_down[l]
    return x


_drawn_inputs = setup_inputs


def setup_inputs(seed=0):
    import zlib

    import numpy as np

    out = dict(_drawn_inputs(seed))
    spreads = {}
    factors = {'q_gain': 8.0, 'k_gain': 8.0, 'r_gain': 5.815, 'conv_b': 5.109, 'ffn_norm': 2.785}
    for name, (base, spread) in spreads.items():
        noise = np.random.default_rng([zlib.crc32(name.encode()), seed]).standard_normal(out[name].shape)
        drawn = base * np.exp(spread * noise) if base else spread * noise
        out[name] = __import__('jax').numpy.asarray(drawn.astype(out[name].dtype))
    for name, factor in factors.items():
        out[name] = (out[name] * factor).astype(out[name].dtype)
    return out
```

```python
import numpy as np
import concourse.bass as bass
from concourse import mybir
from contextlib import ExitStack

P = 128
DEPTH, SEQ, DM, DFF = 2, 256, 2048, 5632
HEADS, HD = 8, 128
WIDTH = HEADS * HD
D_IN = 7 * WIDTH + 2 * DM
REL = 513
EPS = 1e-6
CHUNK = 64
MASKED = -3e38
TT = SEQ // P
NC = 512
UK = 2
IN_BLOCKS, GATE_BLOCKS, UP_BLOCKS = D_IN // NC, 2 * DM // NC, 2 * DFF // NC
Z_BLOCKS = IN_BLOCKS - GATE_BLOCKS
OUT_BLOCKS = DM // NC
KU, KU_BR, KU_DOWN = DM // (UK * P), WIDTH // (UK * P), DFF // (UK * P)
U_IN = 0
U_BR = U_IN + IN_BLOCKS * KU
U_O = U_BR + OUT_BLOCKS * 2 * KU_BR
U_UP = U_O + OUT_BLOCKS * KU
U_DOWN = U_UP + UP_BLOCKS * KU
UNITS = U_DOWN + OUT_BLOCKS * KU_DOWN
N_RAW, N_SPLIT = 4, 2
ACT_BLOCKS = IN_BLOCKS + UP_BLOCKS
DVE_BLOCKS = 4 * OUT_BLOCKS
D_O, D_DOWN = 2 * OUT_BLOCKS, 3 * OUT_BLOCKS
PREPS = 4 * KU
FG = UP_BLOCKS // 2
FT = DFF // P
CONV_ORDER = ([(0, 1), (1, 1), (0, 0), (1, 0), (2, 1), (3, 1), (2, 0), (3, 0)],
              [(0, 1), (1, 1), (0, 0), (1, 0), (2, 1), (3, 1), (2, 0), (3, 0)])

C_ID, C_FLIP, C_COS, C_SIN, C_MASK = 0, P, 2 * P, 3 * P, 4 * P
C_DECAY = C_MASK + 3 * P
C_POW = C_DECAY + HEADS * 4
C_N = C_POW + 4
P_CONV = 0
P_NORM = DEPTH * 2 * FT * 4
P_HEAD = P_NORM + DEPTH * 2 * 16
P_N = P_HEAD + DEPTH * 3


class Steps:

    def __init__(self, sem, names):
        self.sem, self.names, self.at = sem, names.split(), 0

    def done(self, instruction, name):
        assert self.names[self.at % len(self.names)] == name, name
        self.at += 1
        instruction.then_inc(self.sem, 1)

    def after(self, engine, rnd, name):
        engine.wait_ge(self.sem, rnd * len(self.names) + self.names.index(name) + 1)


def trunk(nc, x_in, w_units, consts_in, params_in, rel_in, out):
    f32, f32r = mybir.dt.float32, mybir.dt.float32r
    ALU = mybir.AluOpType
    ACT = mybir.ActivationFunctionType
    AX = mybir.AxisListType
    ds = bass.ds
    ctx = ExitStack()
    with ctx:
        arena_bytes = nc.sbuf_bytes_remaining // 32 * 32 - 64
        arena = ctx.enter_context(nc.sbuf_tensor("arena", [P, arena_bytes // 4], f32))
        base = (nc.sbuf_base - arena_bytes) // 32 * 32 + 32
        at = [base]

        def sb(name, shape, dt=f32, offset=None):
            n = int(np.prod(shape[1:])) * 4
            if offset is None:
                offset = at[0]
                at[0] += (n + 31) // 32 * 32
                assert at[0] <= base + arena_bytes - 64, (name, at[0])
            return nc.alloc_sbuf_tensor_at(name, shape, dt, offset=offset)

        X = sb("X", [P, TT, DM])
        hT_at = at[0]
        HT_hi = sb("HT_hi", [P, 16, SEQ], f32r)
        HT_lo = sb("HT_lo", [P, 16, SEQ], f32r)
        big = at[0]
        GT_hi = sb("GT_hi", [P, FT, SEQ], f32r)
        GT_lo = sb("GT_lo", [P, FT, SEQ], f32r)
        Z = sb("Z", [P, TT, Z_BLOCKS * NC], f32, big)
        GATE = sb("GATE", [P, TT, 2 * DM], f32, big + TT * Z_BLOCKS * NC * 4)
        MT_hi = sb("MT_hi", [P, 16, SEQ], f32r, big)
        MT_lo = sb("MT_lo", [P, 16, SEQ], f32r, big + 16 * SEQ * 4)
        M = sb("M", [P, TT, DM], f32, big + 2 * 16 * SEQ * 4)
        BREV = sb("BREV", [P, HEADS, 2 * P], f32, big)
        ymix = at[0]
        YT = sb("YT", [P, 2 * HEADS, SEQ])
        U = [sb(f"U{j}", [P, TT, NC], f32, ymix + j * 4096) for j in range(2)]
        C = [sb(f"C{j}", [P, 4, SEQ], f32, ymix + 8192 + j * 4096) for j in range(2)]
        RAW = [sb(f"RAW{j}", [P, UK, NC]) for j in range(N_RAW)]
        WH = [sb(f"WH{j}", [P, UK, NC], f32r) for j in range(N_SPLIT)]
        WL = [sb(f"WL{j}", [P, UK, NC], f32r) for j in range(N_SPLIT)]
        K = sb("K", [P, C_N])
        PR = sb("PR", [P, P_N])
        BIAS = sb("BIAS", [P, HEADS, 2 * P])
        SQ = sb("SQ", [P, 4, P])
        QK = sb("QK", [P, 4, P])
        VS = sb("VS", [P, TT, P])
        R1 = sb("R1", [P, TT, 2, P // 2])
        R2 = sb("R2", [P, TT, 2, P // 2])
        RQK = sb("RQK", [P, 4, P])
        QKT = sb("QKT", [P, 4 * P])
        RT = sb("RT", [P, 4 * P])
        SB = sb("SB", [P, 3 * P])
        PT = sb("PT", [P, 3 * P])
        ST = sb("ST", [P, 3 * P])
        SIL = sb("SIL", [P, TT, P])
        YN = sb("YN", [P, TT, P])
        JUNK = sb("JUNK", [P, NC])
        SS = sb("SS", [P, TT, OUT_BLOCKS])
        MSX = sb("MSX", [P, TT])
        RSTD = sb("RSTD", [P, TT])
        NRSTD = sb("NRSTD", [P, TT])
        MSA = sb("MSA", [P, 4])
        MS = sb("MS", [P, 4])
        RS = sb("RS", [P, 4])
        NMX = sb("NMX", [P, 2])
        DEN = sb("DEN", [P, 4])
        YSQ = sb("YSQ", [P, TT])
        YMS = sb("YMS", [P, TT])
        YRS = sb("YRS", [P, 2])

        ident = K[:, C_ID:C_ID + P]
        flip = K[:, C_FLIP:C_FLIP + P]
        cos = K[:, C_COS:C_COS + P].rearrange("p (t o c) -> p t o c", t=TT, o=1).to_broadcast([P, TT, 2, P // 2])
        sin = K[:, C_SIN:C_SIN + P].rearrange("p (t o c) -> p t o c", t=TT, o=1).to_broadcast([P, TT, 2, P // 2])
        mask = K[:, C_MASK:C_MASK + 3 * P]
        minus_half = K[:, C_POW:C_POW + 4]
        Zg = Z[:, :, :].rearrange("p t (g c) -> p t g c", c=HD)

        def norm_gain(l, which, kt):
            return PR[:, ds(P_NORM + l * 32 + which * 16 + kt, 1)]

        def head_gain(l, which):
            return PR[:, ds(P_HEAD + l * 3 + which, 1)]

        def conv_param(l, ft, c):
            return PR[:, ds(l * (2 * FT * 4) + ft * 4 + c, 1)]

        acc = [ctx.enter_context(nc.psum_tensor(f"acc{j}", [P, NC], f32)) for j in range(4)]
        aux = [ctx.enter_context(nc.psum_tensor(f"aux{j}", [P, NC], f32)) for j in range(4)]

        def sem(name):
            return ctx.enter_context(nc.semaphore(name))

        consts_loaded = sem("consts_loaded")
        x_loaded = sem("x_loaded")
        raw_loaded = [sem(f"raw_loaded{j}") for j in range(N_RAW)]
        hi_split = sem("hi_split")
        lo_split = sem("lo_split")
        unit_used = sem("unit_used")
        act_read = sem("act_read")
        dve_read = sem("dve_read")
        prep_T = sem("prep_T")
        prep_hi = sem("prep_hi")
        prep_lo = sem("prep_lo")
        squares = sem("squares")
        bias_flipped = sem("bias_flipped")
        bias_ready = sem("bias_ready")
        norm = Steps(sem("norm"), "sum mean")
        rstd_ready = sem("rstd_ready")
        nrstd_ready = sem("nrstd_ready")
        merged = sem("merged")
        merge = Steps(sem("merge"), "one_a sig_a one_r sig_r")
        pe_h = Steps(sem("pe_h"), "qkT rqkT scores rscores ry pT yT out")
        act_h = Steps(sem("act_h"), "qT kT esil rT exp1 exp0 ysq pT")
        dve_h = Steps(sem("dve_h"), "msa ms qk sil1 sil2 sil sb1 sb0 mx1 mx0 rst den p1 p0 yms yn yr ya")
        pool_h = Steps(sem("pool_h"), "sq rs c1 s1 o1 s2 c2 o2 decay v yrs")
        uT = sem("uT")
        tap = sem("tap")
        conv = sem("conv")
        gelu = sem("gelu")
        product = sem("product")
        g_hi = sem("g_hi")
        g_lo = sem("g_lo")
        stored = sem("stored")
        passed = sem("passed")

        block = ctx.enter_context(nc.Block())

        def used(u):
            return N_SPLIT + u + 1

        def lo_done(u):
            return N_RAW + u + 1

        def dve_has_read(l, d):
            return l * DVE_BLOCKS + d + 3

        def alone(engine):
            engine.sem_inc(passed)

        @block.sync
        def _(sp):
            sp.dma_start(K[:, :], consts_in).then_inc(consts_loaded, 16)
            sp.dma_start(PR[:, :], params_in).then_inc(consts_loaded, 16)
            sp.dma_start(X[:, :, :], x_in.rearrange("b (t p) d -> p (b t) d", p=P)).then_inc(x_loaded, 16)
            rows = bass.AP(tensor=rel_in.tensor, offset=SEQ - P + 1, ap=[[1, P], [REL, HEADS], [1, 2 * P]])
            sp.dma_start(BREV[:, :, :], rows).then_inc(consts_loaded, 16)
            with sp.Fori(0, DEPTH * UNITS // N_RAW) as r:
                for j in range(N_RAW):
                    sp.wait_ge(lo_split, r * N_RAW + j + 1)
                    sp.dma_start(RAW[j][:, :, :],
                                 w_units[ds(r * N_RAW + j, 1), :, :].rearrange("u p (k n) -> (u p) k n", k=UK)
                                 ).then_inc(raw_loaded[j], 16)
            xo = out.rearrange("b (t p) d -> p (b t) d", p=P)
            for nb in range(OUT_BLOCKS):
                sp.wait_ge(dve_read, dve_has_read(DEPTH - 1, D_DOWN + nb))
                sp.dma_start(xo[:, :, nb * NC:(nb + 1) * NC], X[:, :, nb * NC:(nb + 1) * NC]).then_inc(stored, 16)
            sp.wait_ge(stored, 16 * OUT_BLOCKS)

        @block.tensor
        def _(pe):
            mm = nc.tensor.matmul

            def unit(u, s, pair, hi, lo, k0, first, last):
                pe.wait_ge(lo_split, lo_done(u))
                wh, wl = WH[s % N_SPLIT], WL[s % N_SPLIT]
                for kk in range(UK):
                    for t in range(TT):
                        a = acc[2 * pair + t][:, :]
                        h = hi[:, k0 + kk, t * P:(t + 1) * P]
                        mm(a, h, wh[:, kk, :], start=first and kk == 0, stop=False)
                        mm(a, h, wl[:, kk, :], start=False, stop=False)
                        i = mm(a, lo[:, k0 + kk, t * P:(t + 1) * P], wh[:, kk, :], start=False,
                               stop=last and kk == UK - 1)
                i.then_inc(unit_used, 1)

            def transposes(n, j, src):
                if j >= 4:
                    pe.wait_ge(prep_lo, n - 4 + 1)
                for kk in range(UK):
                    for t in range(TT):
                        c = (kk * TT + t) * P
                        i = nc.tensor.transpose(aux[j % 4][:, c:c + P],
                                                src[:, t, (2 * j + kk) * P:(2 * j + kk + 1) * P], ident)
                i.then_inc(prep_T, 1)

            def prepared_block(u, n, pair, src, ready, hi, lo):
                for j in range(3):
                    if ready:
                        ready(j)
                    transposes(n + j, j, src)
                for s in range(KU):
                    pe.wait_ge(prep_lo, n + s + 1)
                    unit(u + s, s, pair, hi, lo, UK * s, s == 0, s == KU - 1)
                    if s + 3 < KU:
                        if ready:
                            ready(s + 3)
                        transposes(n + s + 3, s + 3, src)

            pe.sem_inc(unit_used, N_SPLIT)
            pe.wait_ge(consts_loaded, 48)
            for h in range(HEADS):
                for j in range(2):
                    c = (h % 2) * 2 * P + (1 - j) * P
                    i = mm(aux[h // 2][:, c:c + P], BREV[:, h, j * P:(j + 1) * P], flip, start=True, stop=True)
            i.then_inc(bias_flipped, 1)

            with pe.Fori(0, DEPTH) as l:
                U0, A0, D0, N0 = l * UNITS, l * ACT_BLOCKS, l * DVE_BLOCKS, l * PREPS
                pe.wait_ge(dve_read, D0 + 2)
                pe.wait_ge(bias_ready, 1)
                prepared_block(U0, N0, 0, X, None, HT_hi, HT_lo)
                for s in range(KU):
                    unit(U0 + KU + s, s, 1, HT_hi, HT_lo, UK * s, s == 0, s == KU - 1)
                with pe.Fori(1, Z_BLOCKS // 2) as i:
                    for pair in range(2):
                        pe.wait_ge(act_read, A0 + 2 * i + pair - 1)
                        for s in range(KU):
                            unit(U0 + (2 * i + pair) * KU + s, s, pair, HT_hi, HT_lo, UK * s, s == 0, s == KU - 1)
                with pe.Fori(0, GATE_BLOCKS // 2) as i:
                    for pair in range(2):
                        h = 2 * i + pair
                        n = l * HEADS + h
                        pe.wait_ge(act_read, A0 + Z_BLOCKS + h - 1)
                        for s in range(KU):
                            unit(U0 + (Z_BLOCKS + h) * KU + s, s, pair, HT_hi, HT_lo, UK * s, s == 0, s == KU - 1)
                            if s == 1:
                                dve_h.after(pe, n, "qk")
                                for w in range(2):
                                    for t in range(TT):
                                        c = (2 * w + t) * P
                                        x = nc.tensor.transpose(aux[0][:, c:c + P], QK[:, 2 * t + w, :], ident)
                                pe_h.done(x, "qkT")
                            if s == 2:
                                pool_h.after(pe, n, "decay")
                                for w in range(2):
                                    for t in range(TT):
                                        c = (2 * w + t) * P
                                        x = nc.tensor.transpose(aux[2][:, c:c + P], RQK[:, 2 * t + w, :], ident)
                                pe_h.done(x, "rqkT")
                            if s == 3:
                                act_h.after(pe, n, "kT")
                                mm(aux[1][:, 0:2 * P], QKT[:, P:2 * P], QKT[:, 2 * P:4 * P], start=True, stop=True)
                                x = mm(aux[1][:, 2 * P:3 * P], QKT[:, 0:P], QKT[:, 2 * P:3 * P], start=True, stop=True)
                                pe_h.done(x, "scores")
                            if s == 4:
                                act_h.after(pe, n, "rT")
                                mm(aux[3][:, 0:2 * P], RT[:, 2 * P:3 * P], RT[:, 0:2 * P], start=True, stop=True)
                                x = mm(aux[3][:, 2 * P:3 * P], RT[:, 3 * P:4 * P], RT[:, P:2 * P], start=True, stop=True)
                                pe_h.done(x, "rscores")
                            if s == 5:
                                dve_h.after(pe, n, "rst")
                                rv = [Z[:, t, ds(5 * WIDTH + h * HD, HD)] for t in range(TT)]
                                mm(aux[2][:, 0:P], ST[:, 0:P], rv[0], start=True, stop=True)
                                mm(aux[2][:, P:2 * P], ST[:, P:2 * P], rv[0], start=True, stop=False)
                                x = mm(aux[2][:, P:2 * P], ST[:, 2 * P:3 * P], rv[1], start=False, stop=True)
                                pe_h.done(x, "ry")
                            if s == 6:
                                dve_h.after(pe, n, "p0")
                                nc.tensor.transpose(aux[0][:, 0:P], SB[:, 2 * P:3 * P], ident)
                                nc.tensor.transpose(aux[0][:, P:2 * P], SB[:, 0:P], ident)
                                x = nc.tensor.transpose(aux[0][:, 2 * P:3 * P], SB[:, P:2 * P], ident)
                                pe_h.done(x, "pT")
                            if s == 7:
                                dve_h.after(pe, n, "yn")
                                for t in range(TT):
                                    x = nc.tensor.transpose(aux[3][:, t * P:(t + 1) * P], YN[:, t, :], ident)
                                pe_h.done(x, "yT")
                                act_h.after(pe, n, "pT")
                                pool_h.after(pe, n, "v")
                                mm(aux[1][:, 0:2 * P], VS[:, 0, :], PT[:, 0:2 * P], start=True, stop=False)
                                x = mm(aux[1][:, P:2 * P], VS[:, 1, :], PT[:, 2 * P:3 * P], start=False, stop=True)
                                pe_h.done(x, "out")
                for b in range(2):
                    pe.wait_ge(act_read, A0 + IN_BLOCKS - 1 + b)
                    for s in range(KU_BR):
                        pe.wait_ge(prep_lo, N0 + KU + b * KU_BR + s + 1)
                        unit(U0 + U_BR + b * KU_BR + s, s, b, HT_hi, HT_lo, b * HEADS + UK * s, s == 0, s == KU_BR - 1)
                with pe.Fori(1, OUT_BLOCKS) as nb:
                    for b in range(2):
                        pe.wait_ge(dve_read, D0 + 2 * nb + b + 1)
                        for s in range(KU_BR):
                            unit(U0 + U_BR + (2 * nb + b) * KU_BR + s, s, b, HT_hi, HT_lo, b * HEADS + UK * s,
                                 s == 0, s == KU_BR - 1)

                def m_ready(j):
                    pe.wait_ge(merged, l * OUT_BLOCKS + j // 2 + 1)

                pe.wait_ge(dve_read, D0 + D_O + 1)
                prepared_block(U0 + U_O, N0 + 2 * KU, 0, M, m_ready, MT_hi, MT_lo)
                for nb in range(1, OUT_BLOCKS):
                    pe.wait_ge(dve_read, D0 + D_O + nb + 1)
                    for s in range(KU):
                        unit(U0 + U_O + nb * KU + s, s, nb % 2, MT_hi, MT_lo, UK * s, s == 0, s == KU - 1)

                def x_ready(j):
                    pe.wait_ge(dve_read, dve_has_read(l, D_O + j // 2))

                def up_transposes(n, side, a_block):
                    pe.wait_ge(act_read, a_block)
                    for f in range(4):
                        for t in range(TT):
                            c = ((f % 2) * TT + t) * P
                            x = nc.tensor.transpose(aux[2 * side + f // 2][:, c:c + P],
                                                    U[side][:, t, f * P:(f + 1) * P], ident)
                    x.then_inc(uT, 1)

                pe.wait_ge(dve_read, D0 + D_O + OUT_BLOCKS + 1)
                prepared_block(U0 + U_UP, N0 + 3 * KU, 0, X, x_ready, HT_hi, HT_lo)

                def up_block(c, pair, wait):
                    wait()
                    for s in range(KU):
                        unit(U0 + U_UP + c * KU + s, s, pair, HT_hi, HT_lo, UK * s, s == 0, s == KU - 1)
                        if s == 1:
                            up_transposes(l * UP_BLOCKS + c - 1, 1 - pair, A0 + IN_BLOCKS + c)

                pe.wait_ge(dve_read, D0 + D_O + OUT_BLOCKS + 2)
                alone(pe)
                with pe.Fori(0, FG - 1) as i:
                    up_block(2 * i + 1, 1, lambda: pe.wait_ge(act_read, A0 + IN_BLOCKS + 2 * i))
                    up_block(2 * i + 2, 0, lambda: pe.wait_ge(act_read, A0 + IN_BLOCKS + 2 * i + 1))
                up_block(UP_BLOCKS - 1, 1, lambda: pe.wait_ge(act_read, A0 + IN_BLOCKS + UP_BLOCKS - 2))
                up_transposes(l * UP_BLOCKS + UP_BLOCKS - 1, 1, A0 + IN_BLOCKS + UP_BLOCKS)
                pe.wait_ge(g_lo, l * FG + FG - 1)
                alone(pe)
                with pe.Fori(0, OUT_BLOCKS // 2) as i:
                    for pair in range(2):
                        pe.wait_ge(dve_read, D0 + D_DOWN + 2 * i + pair + 1)
                        for s in range(KU_DOWN):
                            if s == KU_DOWN - 2:
                                pe.wait_ge(g_lo, l * FG + FG)
                            unit(U0 + U_DOWN + (2 * i + pair) * KU_DOWN + s, s, pair, GT_hi, GT_lo, UK * s,
                                 s == 0, s == KU_DOWN - 1)

        @block.scalar
        def _(act):
            activation = nc.scalar.activation

            def split(u, s):
                act.wait_ge(raw_loaded[s % N_RAW], (u - s % N_RAW) * (16 // N_RAW) + 16)
                act.wait_ge(unit_used, used(u - N_SPLIT))
                activation(WH[s % N_SPLIT][:, :, :], RAW[s % N_RAW][:, :, :], ACT.Copy).then_inc(hi_split, 1)

            def prep(n, j, gain, hi):
                act.wait_ge(prep_T, n + 1)
                bank = aux[j % 4]
                if gain is None:
                    x = activation(hi[:, UK * j:UK * j + UK, :], bank[:, :].rearrange("p (k n) -> p k n", k=UK),
                                   ACT.Copy)
                else:
                    for kk in range(UK):
                        x = activation(hi[:, UK * j + kk, :], bank[:, kk * SEQ:(kk + 1) * SEQ], ACT.Copy,
                                       scale=gain(UK * j + kk))
                x.then_inc(prep_hi, 1)

            def square(n, j):
                t, nb = j % TT, j // TT
                if j:
                    act.wait_ge(squares, n * KU + j)
                activation(JUNK[:, :], X[:, t, nb * NC:(nb + 1) * NC], ACT.Square,
                           accum_out=SS[:, t, nb:nb + 1]).then_inc(squares, 1)

            with act.Fori(0, DEPTH) as l:
                U0, A0, D0 = l * UNITS, l * ACT_BLOCKS, l * DVE_BLOCKS
                T0, N0 = l * 3 * KU, l * PREPS

                def normed_block(u, s0, T, which, evac_to, nth):
                    gain = lambda kt: norm_gain(l, which, kt)
                    prep(T, 0, gain, HT_hi)
                    for s in range(KU):
                        split(u + s + 1, s0 + s + 1)
                        if s + 1 < KU:
                            prep(T + s + 1, s + 1, gain, HT_hi)
                        if which == 1:
                            act.wait_ge(dve_read, dve_has_read(l, D_O + s // TT))
                        square(l * 2 + which, s)
                    act.wait_ge(rstd_ready, l * 2 + which + 1)
                    evac(u + KU - 1, 0, evac_to, RSTD, ACT.Copy)

                def evac(u, pair, to, scale, func):
                    act.wait_ge(unit_used, used(u))
                    for t in range(TT):
                        x = activation(to(t), acc[2 * pair + t][:, :], func, scale=scale[:, t:t + 1])
                    x.then_inc(act_read, 1)

                act.wait_ge(dve_read, D0 + 2)
                split(U0, 0)
                normed_block(U0, 0, T0, 0, lambda t: Z[:, t, 0:NC], 0)
                for s in range(KU):
                    split(U0 + KU + s + 1, KU + s + 1)
                evac(U0 + 2 * KU - 1, 1, lambda t: Z[:, t, NC:2 * NC], RSTD, ACT.Copy)
                with act.Fori(1, Z_BLOCKS // 2) as i:
                    for pair in range(2):
                        b = 2 * i + pair
                        for s in range(KU):
                            split(U0 + b * KU + s + 1, s + 1)
                        evac(U0 + b * KU + KU - 1, pair, lambda t: Z[:, t, ds(b * NC, NC)], RSTD, ACT.Copy)
                act.wait_ge(nrstd_ready, l + 1)
                with act.Fori(0, GATE_BLOCKS // 2) as i:
                    for pair in range(2):
                        h = 2 * i + pair
                        n = l * HEADS + h
                        b = Z_BLOCKS + h
                        for s in range(KU):
                            split(U0 + b * KU + s + 1, s + 1)
                            if s == 1:
                                pe_h.after(act, n, "qkT")
                                alone(act)
                                for w, name in ((0, "qT"), (1, "kT")):
                                    act_h.done(activation(QKT[:, w * SEQ:(w + 1) * SEQ],
                                                          aux[0][:, w * SEQ:(w + 1) * SEQ], ACT.Copy,
                                                          scale=head_gain(l, w)), name)
                                act_h.done(activation(SIL[:, :, :], Z[:, :, ds(6 * WIDTH + h * HD, HD)], ACT.Exp,
                                                      scale=-1.0), "esil")
                            if s == 2:
                                pe_h.after(act, n, "rqkT")
                                act_h.done(activation(RT[:, :], aux[2][:, :], ACT.Copy), "rT")
                            if s == 4:
                                dve_h.after(act, n, "mx0")
                                act_h.done(activation(SB[:, 0:2 * P], SB[:, 0:2 * P], ACT.Exp, bias=NMX[:, 0:1],
                                                      accum_out=DEN[:, 0:1]), "exp1")
                                act_h.done(activation(SB[:, 2 * P:3 * P], SB[:, 2 * P:3 * P], ACT.Exp,
                                                      bias=NMX[:, 1:2], accum_out=DEN[:, 1:2]), "exp0")
                            if s == 5:
                                pe_h.after(act, n, "ry")
                                for t in range(TT):
                                    x = activation(JUNK[:, t * P:(t + 1) * P], aux[2][:, t * P:(t + 1) * P], ACT.Square,
                                                   accum_out=YSQ[:, t:t + 1])
                                act_h.done(x, "ysq")
                            if s == 6:
                                pe_h.after(act, n, "pT")
                                act_h.done(activation(PT[:, :], aux[0][:, 0:3 * P], ACT.Copy), "pT")
                        evac(U0 + b * KU + KU - 1, pair, lambda t: GATE[:, t, ds(h * NC, NC)], NRSTD, ACT.Exp)

                def y_hi(j):
                    activation(HT_hi[:, UK * j:UK * j + UK, :], YT[:, UK * j:UK * j + UK, :],
                               ACT.Copy).then_inc(prep_hi, 1)

                dve_h.after(act, l * HEADS + HEADS - 1, "ya")
                act.wait_ge(unit_used, used(U0 + U_BR - 1))
                y_hi(0)
                for s in range(2 * KU_BR):
                    split(U0 + U_BR + s + 1, U_BR + s + 1)
                    if s + 1 < KU:
                        y_hi(s + 1)
                with act.Fori(1, OUT_BLOCKS) as nb:
                    for s in range(2 * KU_BR):
                        split(U0 + U_BR + nb * 2 * KU_BR + s + 1, s + 1)
                prep(T0 + KU, 0, None, MT_hi)
                for s in range(KU):
                    split(U0 + U_O + s + 1, U_O + s + 1)
                    if s + 1 < KU:
                        prep(T0 + KU + s + 1, s + 1, None, MT_hi)
                for s in range(KU, OUT_BLOCKS * KU):
                    split(U0 + U_O + s + 1, U_O + s + 1)

                def taps(g, side, f0):
                    for f in (f0, f0 + 1):
                        ft = side * FT + g * 4 + f
                        activation(C[side][:, f, :], aux[2 * side + f // 2][:, (f % 2) * SEQ:(f % 2 + 1) * SEQ],
                                   ACT.Identity, scale=conv_param(l, ft, 2), bias=conv_param(l, ft, 3)
                                   ).then_inc(tap, 1)

                def up_evac(c, side):
                    evac(U0 + U_UP + c * KU + KU - 1, side, lambda t: U[side][:, t, :], RSTD, ACT.Copy)

                def do_gelu(g):
                    act.wait_ge(conv, (l * FG + g) * 16 + 8)
                    activation(C[0][:, :, :], C[0][:, :, :], ACT.Gelu).then_inc(gelu, 1)

                def b_block(g):
                    for s in range(KU):
                        split(U0 + U_UP + (2 * g + 1) * KU + s + 1, s + 1)
                        if s == 2:
                            act.wait_ge(uT, l * UP_BLOCKS + 2 * g + 1)
                            taps(g, 0, 0)
                        if s == 3:
                            taps(g, 0, 2)
                    up_evac(2 * g + 1, 1)

                def product_hi(g):
                    act.wait_ge(product, l * FG + g + 1)
                    alone(act)
                    activation(GT_hi[:, ds(4 * g, 4), :], C[1][:, :, :], ACT.Copy).then_inc(g_hi, 1)

                normed_block(U0 + U_UP, U_UP, T0 + 2 * KU, 1, lambda t: U[0][:, t, :], 1)
                with act.Fori(0, FG - 1) as g:
                    b_block(g)
                    for s in range(KU):
                        split(U0 + U_UP + (2 * g + 2) * KU + s + 1, s + 1)
                        if s == 0:
                            do_gelu(g)
                        if s == 2:
                            act.wait_ge(uT, l * UP_BLOCKS + 2 * g + 2)
                            taps(g, 1, 0)
                        if s == 3:
                            taps(g, 1, 2)
                    product_hi(g)
                    up_evac(2 * g + 2, 0)
                b_block(FG - 1)
                for s in range(OUT_BLOCKS * KU_DOWN):
                    if s + 1 < OUT_BLOCKS * KU_DOWN:
                        split(U0 + U_DOWN + s + 1, s + 1)
                    if s == 0:
                        do_gelu(FG - 1)
                        act.wait_ge(uT, l * UP_BLOCKS + UP_BLOCKS)
                        taps(FG - 1, 1, 0)
                    if s == 1:
                        taps(FG - 1, 1, 2)
                    if s == KU - 1:
                        product_hi(FG - 1)

        @block.vector
        def _(dve):
            tt, ts, stt = nc.vector.tensor_tensor, nc.vector.tensor_scalar, nc.vector.scalar_tensor_tensor

            def split(u, s):
                dve.wait_ge(hi_split, u + 1)
                tt(WL[s % N_SPLIT][:, :, :], RAW[s % N_RAW][:, :, :], WH[s % N_SPLIT][:, :, :].bitcast(f32),
                   ALU.subtract).then_inc(lo_split, 1)

            def prep(n, j, gain, hi, lo):
                dve.wait_ge(prep_hi, n + 1)
                bank = aux[j % 4]
                if gain is None:
                    x = tt(lo[:, UK * j:UK * j + UK, :], bank[:, :].rearrange("p (k n) -> p k n", k=UK),
                           hi[:, UK * j:UK * j + UK, :].bitcast(f32), ALU.subtract)
                else:
                    for kk in range(UK):
                        x = stt(lo[:, UK * j + kk, :], bank[:, kk * SEQ:(kk + 1) * SEQ], gain(UK * j + kk),
                                hi[:, UK * j + kk, :].bitcast(f32), ALU.mult, ALU.subtract)
                x.then_inc(prep_lo, 1)

            def y_lo(n, j):
                dve.wait_ge(prep_hi, n + 1)
                tt(HT_lo[:, UK * j:UK * j + UK, :], YT[:, UK * j:UK * j + UK, :],
                   HT_hi[:, UK * j:UK * j + UK, :].bitcast(f32), ALU.subtract).then_inc(prep_lo, 1)

            dve.sem_inc(lo_split, N_RAW)
            dve.wait_ge(consts_loaded, 48)
            dve.wait_ge(bias_flipped, 1)
            for h in range(HEADS):
                x = nc.vector.tensor_copy(BIAS[:, h, :], aux[h // 2][:, (h % 2) * 2 * P:(h % 2 + 1) * 2 * P])
            x.then_inc(bias_ready, 1)
            dve.wait_ge(bias_ready, 1)
            nc.vector.memset(BIAS[0:CHUNK, :, P + CHUNK:2 * P], MASKED).then_inc(bias_ready, 1)
            dve.wait_ge(x_loaded, 16)
            dve.sem_inc(dve_read, 2)

            with dve.Fori(0, DEPTH) as l:
                U0, A0, D0, N0 = l * UNITS, l * ACT_BLOCKS, l * DVE_BLOCKS, l * PREPS

                def normed_block(u, s0, n, which):
                    gain = lambda kt: norm_gain(l, which, kt)
                    prep(n, 0, gain, HT_hi, HT_lo)
                    for s in range(KU):
                        split(u + s + 1, s0 + s + 1)
                        if s + 1 < KU:
                            prep(n + s + 1, s + 1, gain, HT_hi, HT_lo)
                    dve.wait_ge(squares, (l * 2 + which + 1) * KU)
                    norm.done(nc.vector.tensor_reduce(MSX[:, :], SS[:, :, :], AX.X, ALU.add), "sum")
                    norm.after(dve, l * 2 + which, "sum")
                    norm.done(ts(MSX[:, :], MSX[:, :], 1.0 / DM, EPS, ALU.mult, ALU.add), "mean")

                def add_to_x(u, pair, nb):
                    dve.wait_ge(unit_used, used(u))
                    for t in range(TT):
                        x = tt(X[:, t, nb * NC:(nb + 1) * NC], acc[2 * pair + t][:, :],
                               X[:, t, nb * NC:(nb + 1) * NC], ALU.add)
                    x.then_inc(dve_read, 1)

                split(U0, 0)
                normed_block(U0, 0, N0, 0)
                for s in range(KU):
                    split(U0 + KU + s + 1, KU + s + 1)
                    if s == 0:
                        dve.wait_ge(rstd_ready, l * 2 + 1)
                        ts(NRSTD[:, :], RSTD[:, :], -1.0, None, ALU.mult).then_inc(nrstd_ready, 1)
                with dve.Fori(1, Z_BLOCKS // 2) as i:
                    for s in range(2 * KU):
                        split(U0 + i * 2 * KU + s + 1, s + 1)
                with dve.Fori(0, GATE_BLOCKS // 2) as i:
                    for pair in range(2):
                        h = 2 * i + pair
                        n = l * HEADS + h
                        for s in range(KU):
                            split(U0 + (Z_BLOCKS + h) * KU + s + 1, s + 1)
                            if s == 0:
                                pool_h.after(dve, n, "sq")
                                dve_h.done(nc.vector.tensor_reduce(MSA[:, :], SQ[:, :, :], AX.X, ALU.add), "msa")
                                dve_h.after(dve, n, "msa")
                                dve_h.done(ts(MS[:, :], MSA[:, :], 1.0 / HD, EPS, ALU.mult, ALU.add), "ms")
                                pool_h.after(dve, n, "rs")
                                dve_h.done(tt(QK[:, :, :].rearrange("p (t w) c -> p t w c", t=TT),
                                              Zg[:, :, ds(h, 2, step=HEADS), :],
                                              RS[:, :].rearrange("p (t w o) -> p t w o", t=TT, o=1)
                                              .to_broadcast([P, TT, 2, HD]), ALU.mult), "qk")
                            if s == 2:
                                act_h.after(dve, n, "esil")
                                dve_h.done(ts(SIL[:, :, :], SIL[:, :, :], 1.0, None, ALU.add), "sil1")
                                dve_h.after(dve, n, "sil1")
                                dve_h.done(nc.vector.reciprocal(SIL[:, :, :], SIL[:, :, :]), "sil2")
                                dve_h.after(dve, n, "sil2")
                                dve_h.done(tt(SIL[:, :, :], SIL[:, :, :], Z[:, :, ds(6 * WIDTH + h * HD, HD)],
                                              ALU.mult), "sil")
                            if s == 3:
                                pe_h.after(dve, n, "scores")
                                dve.wait_ge(bias_ready, 2)
                                bias = BIAS[:, :, :].rearrange("p h c -> p (h c)")
                                dve_h.done(stt(SB[:, 0:2 * P], aux[1][:, 0:2 * P], HD ** -0.5,
                                               bias[:, ds(h * 2 * P, 2 * P)], ALU.mult, ALU.add), "sb1")
                                dve_h.done(stt(SB[:, 2 * P:3 * P], aux[1][:, 2 * P:3 * P], HD ** -0.5,
                                               bias[:, ds(h * 2 * P + P, P)], ALU.mult, ALU.add), "sb0")
                                dve_h.after(dve, n, "sb0")
                                dve_h.done(nc.vector.tensor_reduce(NMX[:, 0:1], SB[:, 0:2 * P], AX.X, ALU.max,
                                                                   negate=True), "mx1")
                                dve_h.done(nc.vector.tensor_reduce(NMX[:, 1:2], SB[:, 2 * P:3 * P], AX.X, ALU.max,
                                                                   negate=True), "mx0")
                            if s == 4:
                                pe_h.after(dve, n, "rscores")
                                dve_h.done(tt(ST[:, :], aux[3][:, 0:3 * P], mask, ALU.mult), "rst")
                            if s == 5:
                                act_h.after(dve, n, "exp0")
                                dve_h.done(nc.vector.reciprocal(DEN[:, 2:4], DEN[:, 0:2]), "den")
                                dve_h.after(dve, n, "den")
                                dve_h.done(ts(SB[:, 0:2 * P], SB[:, 0:2 * P], DEN[:, 2:3], None, ALU.mult), "p1")
                                dve_h.done(ts(SB[:, 2 * P:3 * P], SB[:, 2 * P:3 * P], DEN[:, 3:4], None, ALU.mult),
                                           "p0")
                            if s == 6:
                                act_h.after(dve, n, "ysq")
                                dve_h.done(ts(YMS[:, :], YSQ[:, :], 1.0 / HD, EPS, ALU.mult, ALU.add), "yms")
                                pool_h.after(dve, n, "yrs")
                                for t in range(TT):
                                    x = stt(YN[:, t, :], aux[2][:, t * P:(t + 1) * P], YRS[:, t:t + 1], SIL[:, t, :],
                                            ALU.mult, ALU.mult)
                                dve_h.done(x, "yn")
                            if s == 7:
                                pe_h.after(dve, n, "yT")
                                yt = YT[:, :, :].rearrange("p h s -> p (h s)")
                                dve_h.done(ts(yt[:, ds((HEADS + h) * SEQ, SEQ)], aux[3][:, 0:SEQ], head_gain(l, 2),
                                              None, ALU.mult), "yr")
                                pe_h.after(dve, n, "out")
                                dve_h.done(nc.vector.tensor_copy(yt[:, ds(h * SEQ, SEQ)], aux[1][:, 0:SEQ]), "ya")

                def merge_block(nb, s):
                    n = l * OUT_BLOCKS + nb
                    for side in range(2):
                        g = GATE[:, :, ds(side * DM + nb * NC, NC)]
                        if s == side * KU_BR:
                            if side == 0:
                                dve.wait_ge(act_read, A0 + IN_BLOCKS)
                            merge.done(ts(g, g, 1.0, None, ALU.add), ("one_a", "one_r")[side])
                        if s == side * KU_BR + 1:
                            merge.after(dve, n, ("one_a", "one_r")[side])
                            alone(dve)
                            merge.done(nc.vector.reciprocal(g, g), ("sig_a", "sig_r")[side])
                        if s == side * KU_BR + 3:
                            merge.after(dve, n, ("sig_a", "sig_r")[side])
                            dve.wait_ge(unit_used, used(U0 + U_BR + (2 * nb + side + 1) * KU_BR - 1))
                            for t in range(TT):
                                gt = GATE[:, t, ds(side * DM + nb * NC, NC)]
                                to = gt if side else M[:, t, ds(nb * NC, NC)]
                                x = tt(to, acc[2 * side + t][:, :], gt, ALU.mult)
                            x.then_inc(dve_read, 1)

                y_lo(N0 + KU, 0)
                for s in range(2 * KU_BR):
                    split(U0 + U_BR + s + 1, s + 1)
                    if s + 1 < KU:
                        y_lo(N0 + KU + s + 1, s + 1)
                    merge_block(0, s)
                with dve.Fori(1, OUT_BLOCKS) as nb:
                    for s in range(2 * KU_BR):
                        split(U0 + U_BR + nb * 2 * KU_BR + s + 1, s + 1)
                        merge_block(nb, s)
                prep(N0 + 2 * KU, 0, None, MT_hi, MT_lo)
                for nb in range(OUT_BLOCKS):
                    for s in range(KU):
                        split(U0 + U_O + nb * KU + s + 1, s + 1)
                        if nb == 0 and s + 1 < KU:
                            prep(N0 + 2 * KU + s + 1, s + 1, None, MT_hi, MT_lo)
                    add_to_x(U0 + U_O + nb * KU + KU - 1, nb % 2, nb)

                def conv_tap(g, side, f, k):
                    n = (l * FG + g) * 16 + side * 8
                    order = CONV_ORDER[side]
                    if k == 1:
                        dve.wait_ge(tap, (l * FG + g) * 8 + side * 4 + f // 2 * 2 + 2)
                    else:
                        dve.wait_ge(conv, n + order.index((f, 1)) + 1)
                    back = 2 - k
                    stt(C[side][:, f, back:SEQ], aux[2 * side + f // 2][:, f % 2 * SEQ:(f % 2 + 1) * SEQ - back],
                        conv_param(l, side * FT + g * 4 + f, k), C[side][:, f, back:SEQ],
                        ALU.mult, ALU.add).then_inc(conv, 1)

                def g_low(g):
                    dve.wait_ge(g_hi, l * FG + g + 1)
                    alone(dve)
                    tt(GT_lo[:, ds(4 * g, 4), :], C[1][:, :, :], GT_hi[:, ds(4 * g, 4), :].bitcast(f32),
                       ALU.subtract).then_inc(g_lo, 1)

                def b_block(g):
                    for s in range(KU):
                        split(U0 + U_UP + (2 * g + 1) * KU + s + 1, s + 1)
                        if 3 <= s < 7:
                            for f, k in CONV_ORDER[0][2 * (s - 3):2 * (s - 2)]:
                                conv_tap(g, 0, f, k)

                normed_block(U0 + U_UP, 0, N0 + 3 * KU, 1)
                with dve.Fori(0, FG - 1) as g:
                    b_block(g)
                    for s in range(KU):
                        split(U0 + U_UP + (2 * g + 2) * KU + s + 1, s + 1)
                        if 3 <= s < 6:
                            for f, k in CONV_ORDER[1][3 * (s - 3):3 * (s - 2)]:
                                conv_tap(g, 1, f, k)
                    g_low(g)
                b_block(FG - 1)
                for s in range(OUT_BLOCKS * KU_DOWN):
                    if s + 1 < OUT_BLOCKS * KU_DOWN:
                        split(U0 + U_DOWN + s + 1, s + 1)
                    if 1 <= s < 4:
                        for f, k in CONV_ORDER[1][3 * (s - 1):3 * s]:
                            conv_tap(FG - 1, 1, f, k)
                    if s == KU - 1:
                        g_low(FG - 1)
                    nb, last = divmod(s, KU_DOWN)
                    if last == KU_DOWN - 1:
                        add_to_x(U0 + U_DOWN + s, nb % 2, nb)

        @block.gpsimd
        def _(pool):
            tt = nc.gpsimd.tensor_tensor

            def power(to, of):
                return tt(to, of, minus_half[:, 0:of.shape[1]], ALU.pow)

            pool.wait_ge(consts_loaded, 48)
            with pool.Fori(0, DEPTH) as l:
                norm.after(pool, l * 2, "mean")
                power(RSTD[:, :], MSX[:, :]).then_inc(rstd_ready, 1)
                with pool.Fori(0, HEADS) as h:
                    n = l * HEADS + h
                    pool.wait_ge(act_read, l * ACT_BLOCKS + Z_BLOCKS)
                    zqk = Zg[:, :, ds(h, 2, step=HEADS), :]
                    pool_h.done(tt(SQ[:, :, :].rearrange("p (t w) c -> p t w c", t=TT), zqk, zqk, ALU.mult), "sq")
                    dve_h.after(pool, n, "ms")
                    pool_h.done(power(RS[:, :], MS[:, :]), "rs")
                    z1 = Zg[:, :, ds(3 * HEADS + h, 2, step=HEADS), 0:HD // 2]
                    z2 = Zg[:, :, ds(3 * HEADS + h, 2, step=HEADS), HD // 2:HD]
                    rot = RQK[:, :, :].rearrange("p (t w) c -> p t w c", t=TT)
                    pool_h.done(tt(R1[:, :, :, :], z1, cos, ALU.mult), "c1")
                    pool_h.done(tt(R2[:, :, :, :], z2, sin, ALU.mult), "s1")
                    pool_h.after(pool, n, "s1")
                    pool_h.done(tt(rot[:, :, :, 0:HD // 2], R1[:, :, :, :], R2[:, :, :, :], ALU.subtract), "o1")
                    pool_h.after(pool, n, "o1")
                    alone(pool)
                    pool_h.done(tt(R1[:, :, :, :], z1, sin, ALU.mult), "s2")
                    pool_h.done(tt(R2[:, :, :, :], z2, cos, ALU.mult), "c2")
                    pool_h.after(pool, n, "c2")
                    pool_h.done(tt(rot[:, :, :, HD // 2:HD], R1[:, :, :, :], R2[:, :, :, :], ALU.add), "o2")
                    pool_h.after(pool, n, "o2")
                    pool_h.done(tt(RQK[:, :, :], RQK[:, :, :],
                                   K[:, ds(C_DECAY + h * 4, 4)].rearrange("p (a o) -> p a o", o=1)
                                   .to_broadcast([P, 4, HD]), ALU.mult), "decay")
                    pool_h.done(nc.gpsimd.tensor_copy(VS[:, :, :], Z[:, :, ds(2 * WIDTH + h * HD, HD)]), "v")
                    dve_h.after(pool, n, "yms")
                    pool_h.done(power(YRS[:, :], YMS[:, :]), "yrs")
                with pool.Fori(0, OUT_BLOCKS) as nb:
                    pool.wait_ge(dve_read, l * DVE_BLOCKS + 2 * nb + 4)
                    m = M[:, :, ds(nb * NC, NC)]
                    tt(m, m, GATE[:, :, ds(DM + nb * NC, NC)], ALU.add).then_inc(merged, 1)
                norm.after(pool, l * 2 + 1, "mean")
                power(RSTD[:, :], MSX[:, :]).then_inc(rstd_ready, 1)
                with pool.Fori(0, FG) as g:
                    pool.wait_ge(gelu, l * FG + g + 1)
                    pool.wait_ge(conv, (l * FG + g) * 16 + 16)
                    tt(C[1][:, :, :], C[0][:, :, :], C[1][:, :, :], ALU.mult).then_inc(product, 1)


def constants():
    k = np.zeros((P, C_N), np.float32)
    k[:, C_ID:C_ID + P] = np.eye(P)
    k[:, C_FLIP:C_FLIP + P] = np.eye(P)[::-1]
    half = HD // 2
    inv = np.float32(10000.0) ** (-np.arange(half, dtype=np.float32) / np.float32(half))
    ang = np.arange(SEQ, dtype=np.float32)[:, None] * inv.astype(np.float32)[None, :]
    for at, f in ((C_COS, np.cos), (C_SIN, np.sin)):
        table = f(ang.astype(np.float64)).astype(np.float32).reshape(TT, P, half)
        k[:, at:at + P] = table.transpose(1, 0, 2).reshape(P, TT * half)
    tri = np.triu(np.ones((P, P)))
    k[:, C_MASK:C_MASK + 3 * P] = np.concatenate([tri, np.ones((P, P)), tri], axis=1)
    tok = np.arange(SEQ).reshape(TT, P).T
    for h in range(HEADS):
        lg = np.log1p(-2.0 ** (-5.0 - h))
        for t in range(TT):
            k[:, C_DECAY + h * 4 + 2 * t] = np.exp(lg * tok[:, t])
            k[:, C_DECAY + h * 4 + 2 * t + 1] = np.exp(-lg * tok[:, t]) * HD ** -0.5
    k[:, C_POW:C_POW + 4] = -0.5
    return k


def weight_units(w_in, w_br, w_o, w_up, w_down):
    n = NC
    parts = [
        w_in.reshape(DEPTH, KU, UK, P, IN_BLOCKS, n).transpose(0, 4, 1, 3, 2, 5),
        w_br.reshape(DEPTH, 2, KU_BR, UK, P, OUT_BLOCKS, n).transpose(0, 5, 1, 2, 4, 3, 6),
        w_o.reshape(DEPTH, KU, UK, P, OUT_BLOCKS, n).transpose(0, 4, 1, 3, 2, 5),
        w_up.reshape(DEPTH, KU, UK, P, 2, FG, n).transpose(0, 5, 4, 1, 3, 2, 6),
        w_down.reshape(DEPTH, KU_DOWN, UK, P, OUT_BLOCKS, n).transpose(0, 4, 1, 3, 2, 5),
    ]
    return np.concatenate([p.reshape(DEPTH, -1, P, UK * n) for p in parts], axis=1).reshape(-1, P, UK * n)


def parameters(conv_w, conv_b, mix_norm, ffn_norm, q_gain, k_gain, r_gain):
    conv = np.concatenate([conv_w, conv_b[:, None]], axis=1)
    conv = conv.reshape(DEPTH, 4, 2 * FT, P).transpose(3, 0, 2, 1).reshape(P, -1)
    norms = np.stack([mix_norm, ffn_norm], axis=1).reshape(DEPTH, 2, 16, P).transpose(3, 0, 1, 2).reshape(P, -1)
    heads = np.stack([q_gain, k_gain, r_gain], axis=1).transpose(2, 0, 1).reshape(P, -1)
    return np.concatenate([conv, norms, heads], axis=1)


def kernel(**inputs):
    import concourse.bacc as _bacc
    from concourse import mybir as _mybir
    from concourse.bass_utils import run_bass_kernel_spmd as _run

    a = {k: np.asarray(v) for k, v in inputs.items()}
    arrays = {
        "in_x": a["x"],
        "in_weights": weight_units(a["w_in"], a["w_br"], a["w_o"], a["w_up"], a["w_down"]),
        "in_constants": constants(),
        "in_parameters": parameters(a["conv_w"], a["conv_b"], a["mix_norm"], a["ffn_norm"],
                                    a["q_gain"], a["k_gain"], a["r_gain"]),
        "in_rel_bias": a["rel_bias"],
    }
    arrays = {k: np.ascontiguousarray(v) for k, v in arrays.items()}
    nc = _bacc.Bacc("TRN2", target_bir_lowering=False, num_devices=1, dynamic_dma_scratch_size=1024)
    args = [nc.dram_tensor(k, v.shape, _mybir.dt.from_np(v.dtype), kind="ExternalInput").ap()
            for k, v in arrays.items()]
    out = nc.dram_tensor("out", a["x"].shape, _mybir.dt.from_np(a["x"].dtype), kind="ExternalOutput").ap()
    trunk(nc, *args, out)
    r = _run(nc, [arrays], core_ids=[0])
    return r.results[0]["out"]
```

```python
import numpy as np
import concourse.bass as bass
from concourse import mybir
from contextlib import ExitStack

P = 128
DEPTH, SEQ, DM, DFF = 2, 256, 2048, 5632
HEADS, HD = 8, 128
WIDTH = HEADS * HD
D_IN = 7 * WIDTH + 2 * DM
REL = 513
EPS = 1e-6
CHUNK = 64
MASKED = -3e38
TT = SEQ // P
NC = 512
UK = 2
IN_BLOCKS, GATE_BLOCKS, UP_BLOCKS = D_IN // NC, 2 * DM // NC, 2 * DFF // NC
Z_BLOCKS = IN_BLOCKS - GATE_BLOCKS
OUT_BLOCKS = DM // NC
KU, KU_BR, KU_DOWN = DM // (UK * P), WIDTH // (UK * P), DFF // (UK * P)
U_IN = 0
U_BR = U_IN + IN_BLOCKS * KU
U_O = U_BR + OUT_BLOCKS * 2 * KU_BR
U_UP = U_O + OUT_BLOCKS * KU
U_DOWN = U_UP + UP_BLOCKS * KU
UNITS = U_DOWN + OUT_BLOCKS * KU_DOWN
N_RAW, N_SPLIT = 4, 4
AHEAD = N_SPLIT - 1
ACT_BLOCKS = IN_BLOCKS + UP_BLOCKS
DVE_BLOCKS = 4 * OUT_BLOCKS
D_O, D_DOWN = 2 * OUT_BLOCKS, 3 * OUT_BLOCKS
PREPS = 4 * KU
FG = UP_BLOCKS // 2
FT = DFF // P
CONV_ORDER = ([(0, 1), (1, 1), (0, 0), (1, 0), (2, 1), (3, 1), (2, 0), (3, 0)],
              [(0, 1), (1, 1), (0, 0), (1, 0), (2, 1), (3, 1), (2, 0), (3, 0)])

C_ID, C_FLIP, C_COS, C_SIN, C_MASK = 0, P, 2 * P, 3 * P, 4 * P
C_DECAY = C_MASK + 3 * P
C_POW = C_DECAY + HEADS * 4
C_N = C_POW + 4
P_NORM = 0
P_HEAD = P_NORM + DEPTH * 2 * 16
P_CONV = P_HEAD + DEPTH * 3
P_N = P_CONV + DEPTH * 2 * FT * 4


class Steps:

    def __init__(self, sem, names):
        self.sem, self.names, self.at = sem, names.split(), 0

    def done(self, instruction, name):
        assert self.names[self.at % len(self.names)] == name, name
        self.at += 1
        instruction.then_inc(self.sem, 1)

    def after(self, engine, rnd, name):
        engine.wait_ge(self.sem, rnd * len(self.names) + self.names.index(name) + 1)


def trunk(nc, x_in, w_units, consts_in, params_in, rel_in, out):
    f32, f32r = mybir.dt.float32, mybir.dt.float32r
    ALU = mybir.AluOpType
    ACT = mybir.ActivationFunctionType
    AX = mybir.AxisListType
    ds = bass.ds
    ctx = ExitStack()
    with ctx:
        arena_bytes = nc.sbuf_bytes_remaining // 32 * 32 - 64
        arena = ctx.enter_context(nc.sbuf_tensor("arena", [P, arena_bytes // 4], f32))
        base = (nc.sbuf_base - arena_bytes) // 32 * 32 + 32
        at = [base]

        def sb(name, shape, dt=f32, offset=None):
            n = int(np.prod(shape[1:])) * 4
            if offset is None:
                offset = at[0]
                at[0] += (n + 31) // 32 * 32
                assert at[0] <= base + arena_bytes - 64, (name, at[0])
            return nc.alloc_sbuf_tensor_at(name, shape, dt, offset=offset)

        X = sb("X", [P, TT, DM])
        hT_at = at[0]
        HT_hi = sb("HT_hi", [P, 16, SEQ], f32r)
        HT_lo = sb("HT_lo", [P, 16, SEQ], f32r)
        big = at[0]
        GT_hi = sb("GT_hi", [P, FT, SEQ], f32r)
        GT_lo = sb("GT_lo", [P, FT, SEQ], f32r)
        Z = sb("Z", [P, TT, Z_BLOCKS * NC], f32, big)
        GATE = sb("GATE", [P, TT, 2 * DM], f32, big + TT * Z_BLOCKS * NC * 4)
        MT_hi = sb("MT_hi", [P, 16, SEQ], f32r, big)
        MT_lo = sb("MT_lo", [P, 16, SEQ], f32r, big + 16 * SEQ * 4)
        M = sb("M", [P, TT, DM], f32, big + (Z_BLOCKS * NC + 2 * WIDTH) * 4)
        BREV = sb("BREV", [P, HEADS, 2 * P], f32, big + TT * Z_BLOCKS * NC * 4)
        RAW = [sb(f"RAW{j}", [P, UK, NC]) for j in range(N_RAW)]
        WH = [sb(f"WH{j}", [P, UK, NC], f32r) for j in range(N_SPLIT)]
        WL = [sb(f"WL{j}", [P, UK, NC], f32r) for j in range(N_SPLIT)]
        K = sb("K", [P, C_N])
        PR = sb("PR", [P, P_N])
        BIAS = sb("BIAS", [P, HEADS, 2 * P])
        heads_at = at[0]
        SQ = sb("SQ", [P, 4, P])
        QK = sb("QK", [P, 4, P])
        VS = sb("VS", [P, TT, P])
        R1 = sb("R1", [P, TT, 2, P // 2])
        R2 = sb("R2", [P, TT, 2, P // 2])
        RQK = sb("RQK", [P, 4, P])
        QKT = sb("QKT", [P, 4 * P])
        RT = sb("RT", [P, 4 * P])
        SB = sb("SB", [P, 3 * P])
        PT = sb("PT", [P, 3 * P])
        ST = sb("ST", [P, 3 * P])
        YN = sb("YN", [P, TT, P])
        U = [sb(f"U{j}", [P, TT, NC], f32, heads_at + j * 4 * TT * NC) for j in range(2)]
        C = [sb(f"C{j}", [P, 4, SEQ], f32, heads_at + 8 * TT * NC + j * 16 * SEQ) for j in range(2)]
        at[0] = max(at[0], heads_at + 8 * TT * NC + 32 * SEQ)
        JUNK = sb("JUNK", [P, NC])
        SS = sb("SS", [P, TT, OUT_BLOCKS])
        MSX = sb("MSX", [P, TT])
        RSTD = sb("RSTD", [P, TT])
        MSA = sb("MSA", [P, 4])
        MS = sb("MS", [P, 4])
        RS = sb("RS", [P, 4])
        NMX = sb("NMX", [P, 2])
        DEN = sb("DEN", [P, 4])
        YSQ = sb("YSQ", [P, TT])
        YMS = sb("YMS", [P, TT])
        YRS = sb("YRS", [P, 2])

        ident = K[:, C_ID:C_ID + P]
        flip = K[:, C_FLIP:C_FLIP + P]
        cos = K[:, C_COS:C_COS + P].rearrange("p (t o c) -> p t o c", t=TT, o=1).to_broadcast([P, TT, 2, P // 2])
        sin = K[:, C_SIN:C_SIN + P].rearrange("p (t o c) -> p t o c", t=TT, o=1).to_broadcast([P, TT, 2, P // 2])
        mask = K[:, C_MASK:C_MASK + 3 * P]
        minus_half = K[:, C_POW:C_POW + 4]
        Zg = Z[:, :, :].rearrange("p t (g c) -> p t g c", c=HD)

        def heads_out(j):
            return Z[:, :, j * UK * HD:(j + 1) * UK * HD].rearrange("p t (k c) -> p k t c", k=UK)

        def halves(tile, j):
            return tile[:, UK * j:UK * j + UK, :].rearrange("p k (t c) -> p k t c", t=TT)

        def norm_gain(l, which, kt):
            return PR[:, ds(P_NORM + l * 32 + which * 16 + kt, 1)]

        def head_gain(l, which):
            return PR[:, ds(P_HEAD + l * 3 + which, 1)]

        def conv_param(l, ft, c):
            return PR[:, ds(P_CONV + l * (2 * FT * 4) + ft * 4 + c, 1)]

        acc = [ctx.enter_context(nc.psum_tensor(f"acc{j}", [P, NC], f32)) for j in range(4)]
        aux = [ctx.enter_context(nc.psum_tensor(f"aux{j}", [P, NC], f32)) for j in range(4)]

        def bias_bank(h):
            return (aux[2], aux[3], acc[2], acc[3])[h // 2]

        def sem(name):
            return ctx.enter_context(nc.semaphore(name))

        first_loaded = sem("first_loaded")
        rest_loaded = sem("rest_loaded")
        x_loaded = [sem(f"x_loaded{j}") for j in range(OUT_BLOCKS)]
        raw_loaded = [sem(f"raw_loaded{j}") for j in range(N_RAW)]
        hi_split = sem("hi_split")
        lo_split = sem("lo_split")
        unit_used = sem("unit_used")
        act_read = sem("act_read")
        dve_read = sem("dve_read")
        prep_T = sem("prep_T")
        prep_hi = sem("prep_hi")
        prep_lo = sem("prep_lo")
        squares = sem("squares")
        bias_flipped = sem("bias_flipped")
        bias_ready = sem("bias_ready")
        norm = Steps(sem("norm"), "sum mean")
        rstd_ready = sem("rstd_ready")
        silu = sem("silu")
        sigmoid = sem("sigmoid")
        merged = sem("merged")
        pe_h = Steps(sem("pe_h"), "qkT rqkT scores rscores ry pT yT out")
        act_h = Steps(sem("act_h"), "qT kT rT exp1 exp0 ysq pT")
        dve_h = Steps(sem("dve_h"), "msa ms qk sb1 sb0 mx1 mx0 rst den p1 p0 yms yn yr ya")
        pool_h = Steps(sem("pool_h"), "sq c1 s1 o1 s2 c2 o2 decay rs v yrs")
        uT = sem("uT")
        tap = sem("tap")
        conv = sem("conv")
        gelu = sem("gelu")
        product = sem("product")
        g_hi = sem("g_hi")
        g_lo = sem("g_lo")
        stored = sem("stored")
        passed = sem("passed")

        block = ctx.enter_context(nc.Block())

        def used(u):
            return N_SPLIT + u + 1

        def lo_done(u):
            return N_RAW + u + 1

        def dve_has_read(l, d):
            return l * DVE_BLOCKS + d + 3

        def alone(engine):
            engine.sem_inc(passed)

        @block.sync
        def _(sp):
            def load_unit(r, j):
                sp.dma_start(RAW[j][:, :, :],
                             w_units[ds(r * N_RAW + j, 1), :, :].rearrange("u p (k n) -> (u p) k n", k=UK)
                             ).then_inc(raw_loaded[j], 16)

            xi = x_in.rearrange("b (t p) d -> p (b t) d", p=P)
            rows = bass.AP(tensor=rel_in.tensor, offset=SEQ - P + 1, ap=[[1, P], [REL, HEADS], [1, 2 * P]])
            sp.dma_start(K[:, 0:C_COS], consts_in[:, 0:C_COS]).then_inc(first_loaded, 16)
            sp.dma_start(PR[:, 0:P_CONV], params_in[:, 0:P_CONV]).then_inc(first_loaded, 16)
            sp.dma_start(BREV[:, :, :], rows).then_inc(first_loaded, 16)
            for j in range(OUT_BLOCKS):
                sp.dma_start(X[:, :, j * NC:(j + 1) * NC], xi[:, :, j * NC:(j + 1) * NC]).then_inc(x_loaded[j], 16)
                load_unit(0, j)
            sp.dma_start(K[:, C_COS:C_N], consts_in[:, C_COS:C_N]).then_inc(rest_loaded, 16)
            sp.dma_start(PR[:, P_CONV:P_N], params_in[:, P_CONV:P_N]).then_inc(rest_loaded, 16)
            with sp.Fori(1, DEPTH * UNITS // N_RAW) as r:
                for j in range(N_RAW):
                    sp.wait_ge(lo_split, r * N_RAW + j + 1)
                    load_unit(r, j)
            xo = out.rearrange("b (t p) d -> p (b t) d", p=P)
            for nb in range(OUT_BLOCKS):
                sp.wait_ge(dve_read, dve_has_read(DEPTH - 1, D_DOWN + nb))
                sp.dma_start(xo[:, :, nb * NC:(nb + 1) * NC], X[:, :, nb * NC:(nb + 1) * NC]).then_inc(stored, 16)
            sp.wait_ge(stored, 16 * OUT_BLOCKS)

        @block.tensor
        def _(pe):
            mm = nc.tensor.matmul

            def unit(u, s, pair, hi, lo, k0, first, last):
                pe.wait_ge(lo_split, lo_done(u))
                wh, wl = WH[s % N_SPLIT], WL[s % N_SPLIT]
                for kk in range(UK):
                    for t in range(TT):
                        a = acc[2 * pair + t][:, :]
                        h = hi[:, k0 + kk, t * P:(t + 1) * P]
                        mm(a, h, wh[:, kk, :], start=first and kk == 0, stop=False)
                        mm(a, h, wl[:, kk, :], start=False, stop=False)
                        i = mm(a, lo[:, k0 + kk, t * P:(t + 1) * P], wh[:, kk, :], start=False,
                               stop=last and kk == UK - 1)
                i.then_inc(unit_used, 1)

            def transposes(n, j, src):
                if j >= 4:
                    pe.wait_ge(prep_lo, n - 4 + 1)
                for kk in range(UK):
                    for t in range(TT):
                        c = (kk * TT + t) * P
                        i = nc.tensor.transpose(aux[j % 4][:, c:c + P],
                                                src[:, t, (2 * j + kk) * P:(2 * j + kk + 1) * P], ident)
                i.then_inc(prep_T, 1)

            def first_transposes(n, src, ready):
                for j in range(3):
                    ready(j)
                    transposes(n + j, j, src)

            def prepared_block(u, n, pair, src, ready, hi, lo):
                for s in range(KU):
                    pe.wait_ge(prep_lo, n + s + 1)
                    unit(u + s, s, pair, hi, lo, UK * s, s == 0, s == KU - 1)
                    if s + 3 < KU:
                        ready(s + 3)
                        transposes(n + s + 3, s + 3, src)

            pe.sem_inc(unit_used, N_SPLIT)
            pe.wait_ge(first_loaded, 48)
            for h in range(HEADS):
                for j in range(2):
                    c = (h % 2) * 2 * P + (1 - j) * P
                    i = mm(bias_bank(h)[:, c:c + P], BREV[:, h, j * P:(j + 1) * P], flip, start=True, stop=True)
            i.then_inc(bias_flipped, 1)

            with pe.Fori(0, DEPTH) as l:
                U0, A0, D0, N0 = l * UNITS, l * ACT_BLOCKS, l * DVE_BLOCKS, l * PREPS
                pe.wait_ge(dve_read, D0 + 1)

                def x_in_ready(j):
                    pe.wait_ge(x_loaded[j // 2], 16)
                    if j == 2:
                        pe.wait_ge(bias_ready, 1)
                    if j == 6:
                        pe.wait_ge(dve_read, D0 + 2)

                first_transposes(N0, X, x_in_ready)
                prepared_block(U0, N0, 0, X, x_in_ready, HT_hi, HT_lo)
                pe.wait_ge(bias_ready, 2)
                for s in range(KU):
                    unit(U0 + KU + s, s, 1, HT_hi, HT_lo, UK * s, s == 0, s == KU - 1)
                with pe.Fori(1, Z_BLOCKS // 2) as i:
                    for pair in range(2):
                        pe.wait_ge(act_read, A0 + 2 * i + pair - 1)
                        for s in range(KU):
                            unit(U0 + (2 * i + pair) * KU + s, s, pair, HT_hi, HT_lo, UK * s, s == 0, s == KU - 1)
                with pe.Fori(0, GATE_BLOCKS // 2) as i:
                    for pair in range(2):
                        h = 2 * i + pair
                        n = l * HEADS + h
                        pe.wait_ge(act_read, A0 + Z_BLOCKS + h - 1)
                        for s in range(KU):
                            unit(U0 + (Z_BLOCKS + h) * KU + s, s, pair, HT_hi, HT_lo, UK * s, s == 0, s == KU - 1)
                            if s == 2:
                                dve_h.after(pe, n, "qk")
                                for w in range(2):
                                    for t in range(TT):
                                        c = (2 * w + t) * P
                                        x = nc.tensor.transpose(aux[0][:, c:c + P], QK[:, 2 * t + w, :], ident)
                                pe_h.done(x, "qkT")
                            if s == 2:
                                pool_h.after(pe, n, "decay")
                                for w in range(2):
                                    for t in range(TT):
                                        c = (2 * w + t) * P
                                        x = nc.tensor.transpose(aux[2][:, c:c + P], RQK[:, 2 * t + w, :], ident)
                                pe_h.done(x, "rqkT")
                            if s == 3:
                                act_h.after(pe, n, "kT")
                                mm(aux[1][:, 0:2 * P], QKT[:, P:2 * P], QKT[:, 2 * P:4 * P], start=True, stop=True)
                                x = mm(aux[1][:, 2 * P:3 * P], QKT[:, 0:P], QKT[:, 2 * P:3 * P], start=True, stop=True)
                                pe_h.done(x, "scores")
                            if s == 4:
                                act_h.after(pe, n, "rT")
                                mm(aux[3][:, 0:2 * P], RT[:, 2 * P:3 * P], RT[:, 0:2 * P], start=True, stop=True)
                                x = mm(aux[3][:, 2 * P:3 * P], RT[:, 3 * P:4 * P], RT[:, P:2 * P], start=True, stop=True)
                                pe_h.done(x, "rscores")
                            if s == 5:
                                dve_h.after(pe, n, "rst")
                                rv = [Z[:, t, ds(5 * WIDTH + h * HD, HD)] for t in range(TT)]
                                mm(aux[2][:, 0:P], ST[:, 0:P], rv[0], start=True, stop=True)
                                mm(aux[2][:, P:2 * P], ST[:, P:2 * P], rv[0], start=True, stop=False)
                                x = mm(aux[2][:, P:2 * P], ST[:, 2 * P:3 * P], rv[1], start=False, stop=True)
                                pe_h.done(x, "ry")
                            if s == 6:
                                dve_h.after(pe, n, "p0")
                                nc.tensor.transpose(aux[0][:, 0:P], SB[:, 2 * P:3 * P], ident)
                                nc.tensor.transpose(aux[0][:, P:2 * P], SB[:, 0:P], ident)
                                x = nc.tensor.transpose(aux[0][:, 2 * P:3 * P], SB[:, P:2 * P], ident)
                                pe_h.done(x, "pT")
                            if s == 7:
                                dve_h.after(pe, n, "yn")
                                for t in range(TT):
                                    x = nc.tensor.transpose(aux[3][:, t * P:(t + 1) * P], YN[:, t, :], ident)
                                pe_h.done(x, "yT")
                                act_h.after(pe, n, "pT")
                                pool_h.after(pe, n, "v")
                                mm(aux[1][:, 0:2 * P], VS[:, 0, :], PT[:, 0:2 * P], start=True, stop=False)
                                x = mm(aux[1][:, P:2 * P], VS[:, 1, :], PT[:, 2 * P:3 * P], start=False, stop=True)
                                pe_h.done(x, "out")
                for b in range(2):
                    pe.wait_ge(act_read, A0 + IN_BLOCKS - 1 + b)
                    for s in range(KU_BR):
                        pe.wait_ge(prep_lo, N0 + KU + b * KU_BR + s + 1)
                        unit(U0 + U_BR + b * KU_BR + s, s, b, HT_hi, HT_lo, b * HEADS + UK * s, s == 0, s == KU_BR - 1)
                with pe.Fori(1, OUT_BLOCKS) as nb:
                    for b in range(2):
                        pe.wait_ge(dve_read, D0 + 2 * nb + b + 1)
                        for s in range(KU_BR):
                            unit(U0 + U_BR + (2 * nb + b) * KU_BR + s, s, b, HT_hi, HT_lo, b * HEADS + UK * s,
                                 s == 0, s == KU_BR - 1)

                def m_ready(j):
                    pe.wait_ge(merged, l * OUT_BLOCKS + j // 2 + 1)

                pe.wait_ge(dve_read, D0 + D_O + 1)
                first_transposes(N0 + 2 * KU, M, m_ready)
                prepared_block(U0 + U_O, N0 + 2 * KU, 0, M, m_ready, MT_hi, MT_lo)

                def x_ready(j):
                    pe.wait_ge(dve_read, dve_has_read(l, D_O + j // 2))

                for nb in range(1, OUT_BLOCKS):
                    pe.wait_ge(dve_read, D0 + D_O + nb + 1)
                    for s in range(KU):
                        unit(U0 + U_O + nb * KU + s, s, nb % 2, MT_hi, MT_lo, UK * s, s == 0, s == KU - 1)
                        if nb == OUT_BLOCKS - 1 and s == KU - 3:
                            first_transposes(N0 + 3 * KU, X, x_ready)


                def up_transposes(n, side, a_block):
                    pe.wait_ge(act_read, a_block)
                    for f in range(4):
                        for t in range(TT):
                            c = ((f % 2) * TT + t) * P
                            x = nc.tensor.transpose(aux[2 * side + f // 2][:, c:c + P],
                                                    U[side][:, t, f * P:(f + 1) * P], ident)
                    x.then_inc(uT, 1)

                pe.wait_ge(dve_read, D0 + D_O + OUT_BLOCKS + 1)
                prepared_block(U0 + U_UP, N0 + 3 * KU, 0, X, x_ready, HT_hi, HT_lo)

                def up_block(c, pair, wait):
                    wait()
                    for s in range(KU):
                        unit(U0 + U_UP + c * KU + s, s, pair, HT_hi, HT_lo, UK * s, s == 0, s == KU - 1)
                        if s == 1:
                            up_transposes(l * UP_BLOCKS + c - 1, 1 - pair, A0 + IN_BLOCKS + c)

                pe.wait_ge(dve_read, D0 + D_O + OUT_BLOCKS + 2)
                alone(pe)
                with pe.Fori(0, FG - 1) as i:
                    up_block(2 * i + 1, 1, lambda: pe.wait_ge(act_read, A0 + IN_BLOCKS + 2 * i))
                    up_block(2 * i + 2, 0, lambda: pe.wait_ge(act_read, A0 + IN_BLOCKS + 2 * i + 1))
                up_block(UP_BLOCKS - 1, 1, lambda: pe.wait_ge(act_read, A0 + IN_BLOCKS + UP_BLOCKS - 2))
                up_transposes(l * UP_BLOCKS + UP_BLOCKS - 1, 1, A0 + IN_BLOCKS + UP_BLOCKS)
                pe.wait_ge(g_lo, l * FG + FG - 1)
                alone(pe)
                with pe.Fori(0, OUT_BLOCKS // 2) as i:
                    for pair in range(2):
                        pe.wait_ge(dve_read, D0 + D_DOWN + 2 * i + pair + 1)
                        for s in range(KU_DOWN):
                            if s == KU_DOWN - 2:
                                pe.wait_ge(g_lo, l * FG + FG)
                            unit(U0 + U_DOWN + (2 * i + pair) * KU_DOWN + s, pair * KU_DOWN + s, pair, GT_hi, GT_lo, UK * s,
                                 s == 0, s == KU_DOWN - 1)

        @block.scalar
        def _(act):
            activation = nc.scalar.activation

            def split(u, s):
                act.wait_ge(raw_loaded[s % N_RAW], (u - s % N_RAW) * (16 // N_RAW) + 16)
                act.wait_ge(unit_used, used(u - N_SPLIT))
                activation(WH[s % N_SPLIT][:, :, :], RAW[s % N_RAW][:, :, :], ACT.Copy).then_inc(hi_split, 1)

            def prep(n, j, gain, hi):
                act.wait_ge(prep_T, n + 1)
                bank = aux[j % 4]
                if gain is None:
                    x = activation(hi[:, UK * j:UK * j + UK, :], bank[:, :].rearrange("p (k n) -> p k n", k=UK),
                                   ACT.Copy)
                else:
                    for kk in range(UK):
                        x = activation(hi[:, UK * j + kk, :], bank[:, kk * SEQ:(kk + 1) * SEQ], ACT.Copy,
                                       scale=gain(UK * j + kk))
                x.then_inc(prep_hi, 1)

            def square(n, j):
                t, nb = j % TT, j // TT
                if j:
                    act.wait_ge(squares, n * KU + j)
                activation(JUNK[:, :], X[:, t, nb * NC:(nb + 1) * NC], ACT.Square,
                           accum_out=SS[:, t, nb:nb + 1]).then_inc(squares, 1)

            with act.Fori(0, DEPTH) as l:
                U0, A0, D0 = l * UNITS, l * ACT_BLOCKS, l * DVE_BLOCKS
                T0, N0 = l * 3 * KU, l * PREPS

                def normed_block(u, s0, T, which, evac_to, nth):
                    gain = lambda kt: norm_gain(l, which, kt)
                    if which == 0:
                        split(u, s0)
                        prep(T, 0, gain, HT_hi)
                        split(u + 1, s0 + 1)
                        prep(T + 1, 1, gain, HT_hi)
                        split(u + 2, s0 + 2)
                    for s in range(KU):
                        split(u + s + AHEAD, s0 + s + AHEAD)
                        if s + 2 < KU:
                            prep(T + s + 2, s + 2, gain, HT_hi)
                        if which == 0:
                            act.wait_ge(x_loaded[s // TT], 16)
                        else:
                            act.wait_ge(dve_read, dve_has_read(l, D_O + s // TT))
                        square(l * 2 + which, s)
                    act.wait_ge(rstd_ready, l * 2 + which + 1)
                    evac(u + KU - 1, 0, evac_to, RSTD, ACT.Copy)

                def evac(u, pair, to, scale, func):
                    act.wait_ge(unit_used, used(u))
                    for t in range(TT):
                        x = activation(to(t), acc[2 * pair + t][:, :], func, scale=scale[:, t:t + 1])
                    x.then_inc(act_read, 1)

                act.wait_ge(dve_read, D0 + 2)
                normed_block(U0, 0, T0, 0, lambda t: Z[:, t, 0:NC], 0)
                for s in range(KU):
                    split(U0 + KU + s + AHEAD, KU + s + AHEAD)
                evac(U0 + 2 * KU - 1, 1, lambda t: Z[:, t, NC:2 * NC], RSTD, ACT.Copy)
                with act.Fori(1, Z_BLOCKS // 2) as i:
                    for pair in range(2):
                        b = 2 * i + pair
                        for s in range(KU):
                            split(U0 + b * KU + s + AHEAD, s + AHEAD)
                        evac(U0 + b * KU + KU - 1, pair, lambda t: Z[:, t, ds(b * NC, NC)], RSTD, ACT.Copy)
                act.wait_ge(rest_loaded, 32)
                act.wait_ge(act_read, A0 + Z_BLOCKS)
                activation(Z[:, :, 6 * WIDTH:7 * WIDTH], Z[:, :, 6 * WIDTH:7 * WIDTH], ACT.Silu).then_inc(silu, 1)
                with act.Fori(0, GATE_BLOCKS // 2) as i:
                    for pair in range(2):
                        h = 2 * i + pair
                        n = l * HEADS + h
                        b = Z_BLOCKS + h
                        for s in range(KU):
                            split(U0 + b * KU + s + AHEAD, s + AHEAD)
                            if s == 2:
                                pe_h.after(act, n, "qkT")
                                alone(act)
                                for w, name in ((0, "qT"), (1, "kT")):
                                    act_h.done(activation(QKT[:, w * SEQ:(w + 1) * SEQ],
                                                          aux[0][:, w * SEQ:(w + 1) * SEQ], ACT.Copy,
                                                          scale=head_gain(l, w)), name)
                                pe_h.after(act, n, "rqkT")
                                act_h.done(activation(RT[:, :], aux[2][:, :], ACT.Copy), "rT")
                            if s == 4:
                                dve_h.after(act, n, "mx0")
                                act_h.done(activation(SB[:, 0:2 * P], SB[:, 0:2 * P], ACT.Exp, bias=NMX[:, 0:1],
                                                      accum_out=DEN[:, 0:1]), "exp1")
                                act_h.done(activation(SB[:, 2 * P:3 * P], SB[:, 2 * P:3 * P], ACT.Exp,
                                                      bias=NMX[:, 1:2], accum_out=DEN[:, 1:2]), "exp0")
                            if s == 5:
                                pe_h.after(act, n, "ry")
                                for t in range(TT):
                                    x = activation(JUNK[:, t * P:(t + 1) * P], aux[2][:, t * P:(t + 1) * P], ACT.Square,
                                                   accum_out=YSQ[:, t:t + 1])
                                act_h.done(x, "ysq")
                            if s == 6:
                                pe_h.after(act, n, "pT")
                                act_h.done(activation(PT[:, :], aux[0][:, 0:3 * P], ACT.Copy), "pT")
                        evac(U0 + b * KU + KU - 1, pair, lambda t: GATE[:, t, ds(h * NC, NC)], RSTD, ACT.Copy)

                def y_hi(j):
                    activation(halves(HT_hi, j), heads_out(j), ACT.Copy).then_inc(prep_hi, 1)

                def gate_sigmoid(nb, s):
                    for side in range(2):
                        if s == 2 * side:
                            g = GATE[:, :, ds(side * DM + nb * NC, NC)]
                            activation(g, g, ACT.Sigmoid).then_inc(sigmoid, 1)

                dve_h.after(act, l * HEADS + HEADS - 1, "ya")
                act.wait_ge(act_read, A0 + IN_BLOCKS)
                act.wait_ge(unit_used, used(U0 + U_BR - 1))
                y_hi(0)
                y_hi(1)
                for s in range(2 * KU_BR):
                    split(U0 + U_BR + s + AHEAD, U_BR + s + AHEAD)
                    if s + 2 < KU:
                        y_hi(s + 2)
                    gate_sigmoid(0, s)
                with act.Fori(1, OUT_BLOCKS) as nb:
                    for s in range(2 * KU_BR):
                        split(U0 + U_BR + nb * 2 * KU_BR + s + AHEAD, s + AHEAD)
                        gate_sigmoid(nb, s)
                prep(T0 + KU, 0, None, MT_hi)
                prep(T0 + KU + 1, 1, None, MT_hi)
                for s in range(KU):
                    split(U0 + U_O + s + AHEAD, U_O + s + AHEAD)
                    if s + 2 < KU:
                        prep(T0 + KU + s + 2, s + 2, None, MT_hi)
                for s in range(KU, OUT_BLOCKS * KU):
                    split(U0 + U_O + s + AHEAD, U_O + s + AHEAD)
                    if s >= OUT_BLOCKS * KU - 2:
                        j = s - (OUT_BLOCKS * KU - 2)
                        prep(T0 + 2 * KU + j, j, lambda kt: norm_gain(l, 1, kt), HT_hi)

                def taps(g, side, f0):
                    for f in (f0, f0 + 1):
                        ft = side * FT + g * 4 + f
                        activation(C[side][:, f, :], aux[2 * side + f // 2][:, (f % 2) * SEQ:(f % 2 + 1) * SEQ],
                                   ACT.Identity, scale=conv_param(l, ft, 2), bias=conv_param(l, ft, 3)
                                   ).then_inc(tap, 1)

                def up_evac(c, side):
                    evac(U0 + U_UP + c * KU + KU - 1, side, lambda t: U[side][:, t, :], RSTD, ACT.Copy)

                def do_gelu(g):
                    act.wait_ge(conv, (l * FG + g) * 16 + 8)
                    activation(C[0][:, :, :], C[0][:, :, :], ACT.Gelu).then_inc(gelu, 1)

                def b_block(g):
                    for s in range(KU):
                        split(U0 + U_UP + (2 * g + 1) * KU + s + AHEAD, s + AHEAD)
                        if s == 2:
                            act.wait_ge(uT, l * UP_BLOCKS + 2 * g + 1)
                            taps(g, 0, 0)
                        if s == 3:
                            taps(g, 0, 2)
                    up_evac(2 * g + 1, 1)

                def product_hi(g):
                    act.wait_ge(product, l * FG + g + 1)
                    alone(act)
                    activation(GT_hi[:, ds(4 * g, 4), :], C[1][:, :, :], ACT.Copy).then_inc(g_hi, 1)

                normed_block(U0 + U_UP, U_UP, T0 + 2 * KU, 1, lambda t: U[0][:, t, :], 1)
                with act.Fori(0, FG - 1) as g:
                    b_block(g)
                    for s in range(KU):
                        split(U0 + U_UP + (2 * g + 2) * KU + s + AHEAD, s + AHEAD)
                        if s == 0:
                            do_gelu(g)
                        if s == 2:
                            act.wait_ge(uT, l * UP_BLOCKS + 2 * g + 2)
                            taps(g, 1, 0)
                        if s == 3:
                            taps(g, 1, 2)
                    product_hi(g)
                    up_evac(2 * g + 2, 0)
                b_block(FG - 1)
                for s in range(OUT_BLOCKS * KU_DOWN):
                    if s + AHEAD < OUT_BLOCKS * KU_DOWN:
                        split(U0 + U_DOWN + s + AHEAD, s + AHEAD)
                    if s == 0:
                        do_gelu(FG - 1)
                        act.wait_ge(uT, l * UP_BLOCKS + UP_BLOCKS)
                        taps(FG - 1, 1, 0)
                    if s == 1:
                        taps(FG - 1, 1, 2)
                    if s == KU - 1:
                        product_hi(FG - 1)

        @block.vector
        def _(dve):
            tt, ts, stt = nc.vector.tensor_tensor, nc.vector.tensor_scalar, nc.vector.scalar_tensor_tensor

            def split(u, s):
                dve.wait_ge(hi_split, u + 1)
                tt(WL[s % N_SPLIT][:, :, :], RAW[s % N_RAW][:, :, :], WH[s % N_SPLIT][:, :, :].bitcast(f32),
                   ALU.subtract).then_inc(lo_split, 1)

            def prep(n, j, gain, hi, lo):
                dve.wait_ge(prep_hi, n + 1)
                bank = aux[j % 4]
                if gain is None:
                    x = tt(lo[:, UK * j:UK * j + UK, :], bank[:, :].rearrange("p (k n) -> p k n", k=UK),
                           hi[:, UK * j:UK * j + UK, :].bitcast(f32), ALU.subtract)
                else:
                    for kk in range(UK):
                        x = stt(lo[:, UK * j + kk, :], bank[:, kk * SEQ:(kk + 1) * SEQ], gain(UK * j + kk),
                                hi[:, UK * j + kk, :].bitcast(f32), ALU.mult, ALU.subtract)
                x.then_inc(prep_lo, 1)

            def y_lo(n, j):
                dve.wait_ge(prep_hi, n + 1)
                tt(halves(HT_lo, j), heads_out(j), halves(HT_hi, j).bitcast(f32), ALU.subtract).then_inc(prep_lo, 1)

            dve.sem_inc(lo_split, N_RAW)
            dve.sem_inc(dve_read, 2)
            dve.wait_ge(bias_flipped, 1)
            for h in range(HEADS):
                x = nc.vector.tensor_copy(BIAS[:, h, :], bias_bank(h)[:, (h % 2) * 2 * P:(h % 2 + 1) * 2 * P])
                if h in (HEADS // 2 - 1, HEADS - 1):
                    x.then_inc(bias_ready, 1)
            dve.wait_ge(bias_ready, 2)
            nc.vector.memset(BIAS[0:CHUNK, :, P + CHUNK:2 * P], MASKED).then_inc(bias_ready, 1)

            with dve.Fori(0, DEPTH) as l:
                U0, A0, D0, N0 = l * UNITS, l * ACT_BLOCKS, l * DVE_BLOCKS, l * PREPS

                def normed_block(u, s0, n, which):
                    gain = lambda kt: norm_gain(l, which, kt)
                    if which == 0:
                        split(u, s0)
                        prep(n, 0, gain, HT_hi, HT_lo)
                        split(u + 1, s0 + 1)
                        prep(n + 1, 1, gain, HT_hi, HT_lo)
                        split(u + 2, s0 + 2)
                    for s in range(KU):
                        split(u + s + AHEAD, s0 + s + AHEAD)
                        if s + 2 < KU:
                            prep(n + s + 2, s + 2, gain, HT_hi, HT_lo)
                    dve.wait_ge(squares, (l * 2 + which + 1) * KU)
                    norm.done(nc.vector.tensor_reduce(MSX[:, :], SS[:, :, :], AX.X, ALU.add), "sum")
                    norm.after(dve, l * 2 + which, "sum")
                    norm.done(ts(MSX[:, :], MSX[:, :], 1.0 / DM, EPS, ALU.mult, ALU.add), "mean")

                def add_to_x(u, pair, nb):
                    dve.wait_ge(unit_used, used(u))
                    for t in range(TT):
                        x = tt(X[:, t, nb * NC:(nb + 1) * NC], acc[2 * pair + t][:, :],
                               X[:, t, nb * NC:(nb + 1) * NC], ALU.add)
                    x.then_inc(dve_read, 1)

                normed_block(U0, 0, N0, 0)
                for s in range(KU):
                    split(U0 + KU + s + AHEAD, KU + s + AHEAD)
                with dve.Fori(1, Z_BLOCKS // 2) as i:
                    for s in range(2 * KU):
                        split(U0 + i * 2 * KU + s + AHEAD, s + AHEAD)
                dve.wait_ge(rest_loaded, 32)
                with dve.Fori(0, GATE_BLOCKS // 2) as i:
                    for pair in range(2):
                        h = 2 * i + pair
                        n = l * HEADS + h
                        for s in range(KU):
                            split(U0 + (Z_BLOCKS + h) * KU + s + AHEAD, s + AHEAD)
                            if s == 0:
                                pool_h.after(dve, n, "sq")
                                dve_h.done(nc.vector.tensor_reduce(MSA[:, :], SQ[:, :, :], AX.X, ALU.add), "msa")
                                dve_h.after(dve, n, "msa")
                                dve_h.done(ts(MS[:, :], MSA[:, :], 1.0 / HD, EPS, ALU.mult, ALU.add), "ms")
                                pool_h.after(dve, n, "rs")
                                dve_h.done(tt(QK[:, :, :].rearrange("p (t w) c -> p t w c", t=TT),
                                              Zg[:, :, ds(h, 2, step=HEADS), :],
                                              RS[:, :].rearrange("p (t w o) -> p t w o", t=TT, o=1)
                                              .to_broadcast([P, TT, 2, HD]), ALU.mult), "qk")
                            if s == 3:
                                pe_h.after(dve, n, "scores")
                                dve.wait_ge(bias_ready, 3)
                                bias = BIAS[:, :, :].rearrange("p h c -> p (h c)")
                                dve_h.done(stt(SB[:, 0:2 * P], aux[1][:, 0:2 * P], HD ** -0.5,
                                               bias[:, ds(h * 2 * P, 2 * P)], ALU.mult, ALU.add), "sb1")
                                dve_h.done(stt(SB[:, 2 * P:3 * P], aux[1][:, 2 * P:3 * P], HD ** -0.5,
                                               bias[:, ds(h * 2 * P + P, P)], ALU.mult, ALU.add), "sb0")
                                dve_h.after(dve, n, "sb0")
                                dve_h.done(nc.vector.tensor_reduce(NMX[:, 0:1], SB[:, 0:2 * P], AX.X, ALU.max,
                                                                   negate=True), "mx1")
                                dve_h.done(nc.vector.tensor_reduce(NMX[:, 1:2], SB[:, 2 * P:3 * P], AX.X, ALU.max,
                                                                   negate=True), "mx0")
                            if s == 4:
                                pe_h.after(dve, n, "rscores")
                                dve_h.done(tt(ST[:, :], aux[3][:, 0:3 * P], mask, ALU.mult), "rst")
                            if s == 5:
                                act_h.after(dve, n, "exp0")
                                dve_h.done(nc.vector.reciprocal(DEN[:, 2:4], DEN[:, 0:2]), "den")
                                dve_h.after(dve, n, "den")
                                dve_h.done(ts(SB[:, 0:2 * P], SB[:, 0:2 * P], DEN[:, 2:3], None, ALU.mult), "p1")
                                dve_h.done(ts(SB[:, 2 * P:3 * P], SB[:, 2 * P:3 * P], DEN[:, 3:4], None, ALU.mult),
                                           "p0")
                            if s == 6:
                                act_h.after(dve, n, "ysq")
                                dve_h.done(ts(YMS[:, :], YSQ[:, :], 1.0 / HD, EPS, ALU.mult, ALU.add), "yms")
                                dve.wait_ge(silu, l + 1)
                                pool_h.after(dve, n, "yrs")
                                for t in range(TT):
                                    x = stt(YN[:, t, :], aux[2][:, t * P:(t + 1) * P], YRS[:, t:t + 1],
                                            Z[:, t, ds(6 * WIDTH + h * HD, HD)],
                                            ALU.mult, ALU.mult)
                                dve_h.done(x, "yn")
                            if s == 7:
                                pe_h.after(dve, n, "yT")
                                dve_h.done(ts(Zg[:, :, HEADS + h, :], aux[3][:, 0:SEQ].rearrange("p (t c) -> p t c", t=TT),
                                              head_gain(l, 2), None, ALU.mult), "yr")
                                pe_h.after(dve, n, "out")
                                alone(dve)
                                dve_h.done(nc.vector.tensor_copy(
                                    Zg[:, :, h, :], aux[1][:, 0:SEQ].rearrange("p (t c) -> p t c", t=TT)), "ya")

                def merge_block(nb, s):
                    for side in range(2):
                        if s == side * KU_BR + KU_BR - 1:
                            dve.wait_ge(sigmoid, (l * OUT_BLOCKS + nb) * 2 + side + 1)
                            dve.wait_ge(unit_used, used(U0 + U_BR + (2 * nb + side + 1) * KU_BR - 1))
                            for t in range(TT):
                                gt = GATE[:, t, ds(side * DM + nb * NC, NC)]
                                to = gt if side else M[:, t, ds(nb * NC, NC)]
                                x = tt(to, acc[2 * side + t][:, :], gt, ALU.mult)
                            x.then_inc(dve_read, 1)

                y_lo(N0 + KU, 0)
                y_lo(N0 + KU + 1, 1)
                for s in range(2 * KU_BR):
                    split(U0 + U_BR + s + AHEAD, s + AHEAD)
                    if s + 2 < KU:
                        y_lo(N0 + KU + s + 2, s + 2)
                    merge_block(0, s)
                with dve.Fori(1, OUT_BLOCKS) as nb:
                    for s in range(2 * KU_BR):
                        split(U0 + U_BR + nb * 2 * KU_BR + s + AHEAD, s + AHEAD)
                        merge_block(nb, s)
                prep(N0 + 2 * KU, 0, None, MT_hi, MT_lo)
                prep(N0 + 2 * KU + 1, 1, None, MT_hi, MT_lo)
                for nb in range(OUT_BLOCKS):
                    for s in range(KU):
                        split(U0 + U_O + nb * KU + s + AHEAD, s + AHEAD)
                        if nb == 0 and s + 2 < KU:
                            prep(N0 + 2 * KU + s + 2, s + 2, None, MT_hi, MT_lo)
                        if nb == OUT_BLOCKS - 1 and s >= KU - 2:
                            j = s - (KU - 2)
                            prep(N0 + 3 * KU + j, j, lambda kt: norm_gain(l, 1, kt), HT_hi, HT_lo)
                    add_to_x(U0 + U_O + nb * KU + KU - 1, nb % 2, nb)

                def conv_tap(g, side, f, k):
                    n = (l * FG + g) * 16 + side * 8
                    order = CONV_ORDER[side]
                    if k == 1:
                        dve.wait_ge(tap, (l * FG + g) * 8 + side * 4 + f // 2 * 2 + 2)
                    else:
                        dve.wait_ge(conv, n + order.index((f, 1)) + 1)
                    back = 2 - k
                    stt(C[side][:, f, back:SEQ], aux[2 * side + f // 2][:, f % 2 * SEQ:(f % 2 + 1) * SEQ - back],
                        conv_param(l, side * FT + g * 4 + f, k), C[side][:, f, back:SEQ],
                        ALU.mult, ALU.add).then_inc(conv, 1)

                def g_low(g):
                    dve.wait_ge(g_hi, l * FG + g + 1)
                    alone(dve)
                    tt(GT_lo[:, ds(4 * g, 4), :], C[1][:, :, :], GT_hi[:, ds(4 * g, 4), :].bitcast(f32),
                       ALU.subtract).then_inc(g_lo, 1)

                def b_block(g):
                    for s in range(KU):
                        split(U0 + U_UP + (2 * g + 1) * KU + s + AHEAD, s + AHEAD)
                        if 3 <= s < 7:
                            for f, k in CONV_ORDER[0][2 * (s - 3):2 * (s - 2)]:
                                conv_tap(g, 0, f, k)

                normed_block(U0 + U_UP, 0, N0 + 3 * KU, 1)
                with dve.Fori(0, FG - 1) as g:
                    b_block(g)
                    for s in range(KU):
                        split(U0 + U_UP + (2 * g + 2) * KU + s + AHEAD, s + AHEAD)
                        if 3 <= s < 6:
                            for f, k in CONV_ORDER[1][3 * (s - 3):3 * (s - 2)]:
                                conv_tap(g, 1, f, k)
                    g_low(g)
                b_block(FG - 1)
                for s in range(OUT_BLOCKS * KU_DOWN):
                    if s + AHEAD < OUT_BLOCKS * KU_DOWN:
                        split(U0 + U_DOWN + s + AHEAD, s + AHEAD)
                    if 1 <= s < 4:
                        for f, k in CONV_ORDER[1][3 * (s - 1):3 * s]:
                            conv_tap(FG - 1, 1, f, k)
                    if s == KU - 1:
                        g_low(FG - 1)
                    nb, last = divmod(s, KU_DOWN)
                    if last == KU_DOWN - 1:
                        add_to_x(U0 + U_DOWN + s, nb % 2, nb)

        @block.gpsimd
        def _(pool):
            tt = nc.gpsimd.tensor_tensor

            def power(to, of):
                return tt(to, of, minus_half[:, 0:of.shape[1]], ALU.pow)

            pool.wait_ge(rest_loaded, 32)
            with pool.Fori(0, DEPTH) as l:
                norm.after(pool, l * 2, "mean")
                power(RSTD[:, :], MSX[:, :]).then_inc(rstd_ready, 1)
                with pool.Fori(0, HEADS) as h:
                    n = l * HEADS + h
                    pool.wait_ge(act_read, l * ACT_BLOCKS + Z_BLOCKS)
                    zqk = Zg[:, :, ds(h, 2, step=HEADS), :]
                    pool_h.done(tt(SQ[:, :, :].rearrange("p (t w) c -> p t w c", t=TT), zqk, zqk, ALU.mult), "sq")
                    z1 = Zg[:, :, ds(3 * HEADS + h, 2, step=HEADS), 0:HD // 2]
                    z2 = Zg[:, :, ds(3 * HEADS + h, 2, step=HEADS), HD // 2:HD]
                    rot = RQK[:, :, :].rearrange("p (t w) c -> p t w c", t=TT)
                    pool_h.done(tt(R1[:, :, :, :], z1, cos, ALU.mult), "c1")
                    pool_h.done(tt(R2[:, :, :, :], z2, sin, ALU.mult), "s1")
                    pool_h.after(pool, n, "s1")
                    pool_h.done(tt(rot[:, :, :, 0:HD // 2], R1[:, :, :, :], R2[:, :, :, :], ALU.subtract), "o1")
                    pool_h.after(pool, n, "o1")
                    alone(pool)
                    pool_h.done(tt(R1[:, :, :, :], z1, sin, ALU.mult), "s2")
                    pool_h.done(tt(R2[:, :, :, :], z2, cos, ALU.mult), "c2")
                    pool_h.after(pool, n, "c2")
                    pool_h.done(tt(rot[:, :, :, HD // 2:HD], R1[:, :, :, :], R2[:, :, :, :], ALU.add), "o2")
                    pool_h.after(pool, n, "o2")
                    pool_h.done(tt(RQK[:, :, :], RQK[:, :, :],
                                   K[:, ds(C_DECAY + h * 4, 4)].rearrange("p (a o) -> p a o", o=1)
                                   .to_broadcast([P, 4, HD]), ALU.mult), "decay")
                    dve_h.after(pool, n, "ms")
                    pool_h.done(power(RS[:, :], MS[:, :]), "rs")
                    pool_h.done(nc.gpsimd.tensor_copy(VS[:, :, :], Z[:, :, ds(2 * WIDTH + h * HD, HD)]), "v")
                    dve_h.after(pool, n, "yms")
                    pool_h.done(power(YRS[:, :], YMS[:, :]), "yrs")
                with pool.Fori(0, OUT_BLOCKS) as nb:
                    pool.wait_ge(dve_read, l * DVE_BLOCKS + 2 * nb + 4)
                    m = M[:, :, ds(nb * NC, NC)]
                    tt(m, m, GATE[:, :, ds(DM + nb * NC, NC)], ALU.add).then_inc(merged, 1)
                norm.after(pool, l * 2 + 1, "mean")
                power(RSTD[:, :], MSX[:, :]).then_inc(rstd_ready, 1)
                with pool.Fori(0, FG) as g:
                    pool.wait_ge(gelu, l * FG + g + 1)
                    pool.wait_ge(conv, (l * FG + g) * 16 + 16)
                    tt(C[1][:, :, :], C[0][:, :, :], C[1][:, :, :], ALU.mult).then_inc(product, 1)


def constants():
    k = np.zeros((P, C_N), np.float32)
    k[:, C_ID:C_ID + P] = np.eye(P)
    k[:, C_FLIP:C_FLIP + P] = np.eye(P)[::-1]
    half = HD // 2
    inv = np.float32(10000.0) ** (-np.arange(half, dtype=np.float32) / np.float32(half))
    ang = np.arange(SEQ, dtype=np.float32)[:, None] * inv.astype(np.float32)[None, :]
    for at, f in ((C_COS, np.cos), (C_SIN, np.sin)):
        table = f(ang.astype(np.float64)).astype(np.float32).reshape(TT, P, half)
        k[:, at:at + P] = table.transpose(1, 0, 2).reshape(P, TT * half)
    tri = np.triu(np.ones((P, P)))
    k[:, C_MASK:C_MASK + 3 * P] = np.concatenate([tri, np.ones((P, P)), tri], axis=1)
    tok = np.arange(SEQ).reshape(TT, P).T
    for h in range(HEADS):
        lg = np.log1p(-2.0 ** (-5.0 - h))
        for t in range(TT):
            k[:, C_DECAY + h * 4 + 2 * t] = np.exp(lg * tok[:, t])
            k[:, C_DECAY + h * 4 + 2 * t + 1] = np.exp(-lg * tok[:, t]) * HD ** -0.5
    k[:, C_POW:C_POW + 4] = -0.5
    return k


def weight_units(w_in, w_br, w_o, w_up, w_down):
    n = NC
    parts = [
        w_in.reshape(DEPTH, KU, UK, P, IN_BLOCKS, n).transpose(0, 4, 1, 3, 2, 5),
        w_br.reshape(DEPTH, 2, KU_BR, UK, P, OUT_BLOCKS, n).transpose(0, 5, 1, 2, 4, 3, 6),
        w_o.reshape(DEPTH, KU, UK, P, OUT_BLOCKS, n).transpose(0, 4, 1, 3, 2, 5),
        w_up.reshape(DEPTH, KU, UK, P, 2, FG, n).transpose(0, 5, 4, 1, 3, 2, 6),
        w_down.reshape(DEPTH, KU_DOWN, UK, P, OUT_BLOCKS, n).transpose(0, 4, 1, 3, 2, 5),
    ]
    return np.concatenate([p.reshape(DEPTH, -1, P, UK * n) for p in parts], axis=1).reshape(-1, P, UK * n)


def parameters(conv_w, conv_b, mix_norm, ffn_norm, q_gain, k_gain, r_gain):
    conv = np.concatenate([conv_w, conv_b[:, None]], axis=1)
    conv = conv.reshape(DEPTH, 4, 2 * FT, P).transpose(3, 0, 2, 1).reshape(P, -1)
    norms = np.stack([mix_norm, ffn_norm], axis=1).reshape(DEPTH, 2, 16, P).transpose(3, 0, 1, 2).reshape(P, -1)
    heads = np.stack([q_gain, k_gain, r_gain], axis=1).transpose(2, 0, 1).reshape(P, -1)
    return np.concatenate([norms, heads, conv], axis=1)


def kernel(**inputs):
    import concourse.bacc as _bacc
    from concourse import mybir as _mybir
    from concourse.bass_utils import run_bass_kernel_spmd as _run

    a = {k: np.asarray(v) for k, v in inputs.items()}
    arrays = {
        "in_x": a["x"],
        "in_weights": weight_units(a["w_in"], a["w_br"], a["w_o"], a["w_up"], a["w_down"]),
        "in_constants": constants(),
        "in_parameters": parameters(a["conv_w"], a["conv_b"], a["mix_norm"], a["ffn_norm"],
                                    a["q_gain"], a["k_gain"], a["r_gain"]),
        "in_rel_bias": a["rel_bias"],
    }
    arrays = {k: np.ascontiguousarray(v) for k, v in arrays.items()}
    nc = _bacc.Bacc("TRN2", target_bir_lowering=False, num_devices=1, dynamic_dma_scratch_size=1024)
    args = [nc.dram_tensor(k, v.shape, _mybir.dt.from_np(v.dtype), kind="ExternalInput").ap()
            for k, v in arrays.items()]
    out = nc.dram_tensor("out", a["x"].shape, _mybir.dt.from_np(a["x"].dtype), kind="ExternalOutput").ap()
    trunk(nc, *args, out)
    r = _run(nc, [arrays], core_ids=[0])
    return r.results[0]["out"]
```
